# Optimizing a Trainium2 kernel written in Bass

```python
import jax, jax.numpy as jnp
from jax import lax
import numpy as np

D_MODEL = 1024
BATCH = 1
SEQ = 256
DEPTH = 2

CHUNK = 64
Q_BLOCK = 128
RMS_EPS = 1e-6
ROPE_THETA = 10000.0
NEG_INF = -1e30

A_HEADS = 16
A_KV_HEADS = 2
A_GROUP = A_HEADS // A_KV_HEADS
A_HEAD_DIM = 64
A_WINDOW = 128
A_WIN_CHUNKS = A_WINDOW // CHUNK

B_HEADS = 8
B_Q_LORA = 384
B_KV_LORA = 256
B_NOPE = 64
B_ROPE = 32
B_V = 64
B_QK = B_NOPE + B_ROPE

D_FF = 4 * D_MODEL

IN_SPLITS = (A_HEADS * A_HEAD_DIM, A_KV_HEADS * A_HEAD_DIM, A_KV_HEADS * A_HEAD_DIM,
             B_Q_LORA, B_KV_LORA + B_ROPE, D_MODEL, D_MODEL)
IN_COLS = sum(IN_SPLITS)
IN_OFFSETS = tuple(int(v) for v in np.cumsum(IN_SPLITS)[:-1])

kernel_name = "hybrid_swa_sink_mla_gated_encoder"

def rms_norm(x, g):
    xf = x.astype(jnp.float32)
    y = xf * lax.rsqrt(jnp.mean(xf * xf, axis=-1, keepdims=True) + RMS_EPS)
    return (y * g.astype(jnp.float32)).astype(x.dtype)

def rope_angles(positions, dim):
    inv_freq = ROPE_THETA ** (-jnp.arange(0, dim, 2, dtype=jnp.float32) / dim)
    ang = positions.astype(jnp.float32)[..., None] * inv_freq
    return jnp.cos(ang), jnp.sin(ang)

def apply_rope(x, cos, sin):
    c = cos[:, :, None, :]
    s = sin[:, :, None, :]
    xf = x.astype(jnp.float32)
    x1, x2 = jnp.split(xf, 2, axis=-1)
    return jnp.concatenate([x1 * c - x2 * s, x2 * c + x1 * s], axis=-1).astype(x.dtype)

def swa_sink_attention(q, k, v, sinks):
    B, S = q.shape[:2]
    n_chunks = S // CHUNK
    qc = q.reshape(B, n_chunks, CHUNK, A_KV_HEADS, A_GROUP, A_HEAD_DIM)

    def band(t):
        tc = t.reshape(B, n_chunks, CHUNK, A_KV_HEADS, A_HEAD_DIM)
        tp = jnp.pad(tc, ((0, 0), (A_WIN_CHUNKS - 1, 0), (0, 0), (0, 0), (0, 0)))
        return jnp.concatenate([tp[:, j:j + n_chunks] for j in range(A_WIN_CHUNKS)], axis=2)

    kb = band(k)
    vb = band(v)
    key_chunk = (jnp.arange(n_chunks)[:, None] - (A_WIN_CHUNKS - 1)
                 + jnp.repeat(jnp.arange(A_WIN_CHUNKS), CHUNK)[None, :])
    valid = key_chunk >= 0
    scale = A_HEAD_DIM ** -0.5
    s = jnp.einsum('bcqkgd,bcskd->bckgqs', qc, kb).astype(jnp.float32) * scale
    s = jnp.where(valid[None, :, None, None, None, :], s, NEG_INF)
    sink = sinks.astype(jnp.float32).reshape(A_KV_HEADS, A_GROUP)[None, None, :, :, None, None]
    logits = jnp.concatenate([s, jnp.broadcast_to(sink, s.shape[:-1] + (1,))], axis=-1)
    p = jax.nn.softmax(logits, axis=-1)[..., :-1].astype(v.dtype)
    o = jnp.einsum('bckgqs,bcskd->bcqkgd', p, vb)
    return o.reshape(B, S, A_HEADS * A_HEAD_DIM)

def mla_attention(q, k, v):
    B, S = q.shape[:2]
    n_blocks = S // Q_BLOCK
    qb = q.reshape(B, n_blocks, Q_BLOCK, B_HEADS, B_QK).transpose(1, 0, 2, 3, 4)
    key_chunk = jnp.arange(S) // CHUNK
    scale = B_QK ** -0.5

    def block(args):
        qi, i = args
        s = jnp.einsum('bqhd,bkhd->bhqk', qi, k).astype(jnp.float32) * scale
        q_chunk = (i * Q_BLOCK + jnp.arange(Q_BLOCK)) // CHUNK
        mask = key_chunk[None, :] <= q_chunk[:, None]
        s = jnp.where(mask[None, None], s, NEG_INF)
        p = jax.nn.softmax(s, axis=-1).astype(v.dtype)
        return jnp.einsum('bhqk,bkhd->bqhd', p, v)

    o = lax.map(block, (qb, jnp.arange(n_blocks)))
    return o.transpose(1, 0, 2, 3, 4).reshape(B, S, B_HEADS * B_V)

def hybrid_layer(x, cos_a, sin_a, cos_b, sin_b, g_mix_pre, g_mix_post, g_mlp_pre, g_mlp_post,
                 w_in, b_gate, sinks, q_norm, kv_norm, w_uq, w_ukv, w_oa, w_ob, w_out,
                 w_mlp_in, w_mlp_out):
    B, S = x.shape[:2]
    u = rms_norm(x, g_mix_pre)
    proj = u @ w_in
    qa, ka, va, cq, ckv, ga, gb = jnp.split(proj, IN_OFFSETS, axis=-1)

    qa = apply_rope(qa.reshape(B, S, A_HEADS, A_HEAD_DIM), cos_a, sin_a)
    ka = apply_rope(ka.reshape(B, S, A_KV_HEADS, A_HEAD_DIM), cos_a, sin_a)
    va = va.reshape(B, S, A_KV_HEADS, A_HEAD_DIM)
    y_a = swa_sink_attention(qa, ka, va, sinks)

    cq = rms_norm(cq, q_norm)
    qb = (cq @ w_uq).reshape(B, S, B_HEADS, B_QK)
    q_nope, q_pe = jnp.split(qb, [B_NOPE], axis=-1)
    qb = jnp.concatenate([q_nope, apply_rope(q_pe, cos_b, sin_b)], axis=-1)
    c_kv, k_pe = jnp.split(ckv, [B_KV_LORA], axis=-1)
    c_kv = rms_norm(c_kv, kv_norm)
    kv = (c_kv @ w_ukv).reshape(B, S, B_HEADS, B_NOPE + B_V)
    k_nope, vb = jnp.split(kv, [B_NOPE], axis=-1)
    k_pe = apply_rope(k_pe[:, :, None, :], cos_b, sin_b)
    kb = jnp.concatenate([k_nope, jnp.broadcast_to(k_pe, (B, S, B_HEADS, B_ROPE))], axis=-1)
    y_b = mla_attention(qb, kb, vb)

    gate_a = jax.nn.sigmoid(ga + b_gate[0])
    gate_b = jax.nn.sigmoid(gb + b_gate[1])
    mixed = gate_a * (y_a @ w_oa) + gate_b * (y_b @ w_ob)
    x = x + rms_norm(mixed @ w_out, g_mix_post)

    h = rms_norm(x, g_mlp_pre)
    h = jnp.square(jax.nn.relu(h @ w_mlp_in)) @ w_mlp_out
    return x + rms_norm(h, g_mlp_post)

def setup_inputs(seed: int = 0) -> dict:
    key = jax.random.key(seed)
    ks = jax.random.split(key, 24)

    def w(k, shape, fan_in):
        return jax.random.normal(k, shape, jnp.float32) * fan_in ** -0.5

    def gain(k, n):
        return 1.0 + 0.05 * jax.random.normal(k, (DEPTH, n), jnp.float32)

    x = jax.random.normal(ks[0], (BATCH, SEQ, D_MODEL), jnp.float32)
    positions = jnp.broadcast_to(jnp.arange(SEQ, dtype=jnp.int32)[None, :], (BATCH, SEQ))
    return {
        "x": x,
        "positions": positions,
        "g_mix_pre": gain(ks[1], D_MODEL),
        "g_mix_post": gain(ks[2], D_MODEL),
        "g_mlp_pre": gain(ks[3], D_MODEL),
        "g_mlp_post": gain(ks[4], D_MODEL),
        "w_in": w(ks[5], (DEPTH, D_MODEL, IN_COLS), D_MODEL),
        "b_gate": 0.1 * jax.random.normal(ks[6], (DEPTH, 2, D_MODEL), jnp.float32),
        "sinks": 0.5 * jax.random.normal(ks[7], (DEPTH, A_HEADS), jnp.float32),
        "q_norm": gain(ks[8], B_Q_LORA),
        "kv_norm": gain(ks[9], B_KV_LORA),
        "w_uq": w(ks[10], (DEPTH, B_Q_LORA, B_HEADS * B_QK), B_Q_LORA),
        "w_ukv": w(ks[11], (DEPTH, B_KV_LORA, B_HEADS * (B_NOPE + B_V)), B_KV_LORA),
        "w_oa": w(ks[12], (DEPTH, A_HEADS * A_HEAD_DIM, D_MODEL), A_HEADS * A_HEAD_DIM),
        "w_ob": w(ks[13], (DEPTH, B_HEADS * B_V, D_MODEL), B_HEADS * B_V),
        "w_out": w(ks[14], (DEPTH, D_MODEL, D_MODEL), D_MODEL),
        "w_mlp_in": w(ks[15], (DEPTH, D_MODEL, D_FF), D_MODEL),
        "w_mlp_out": w(ks[16], (DEPTH, D_FF, D_MODEL), D_FF),
    }

def reference(x, positions, g_mix_pre, g_mix_post, g_mlp_pre, g_mlp_post, w_in, b_gate, sinks,
              q_norm, kv_norm, w_uq, w_ukv, w_oa, w_ob, w_out, w_mlp_in, w_mlp_out):
    cos_a, sin_a = rope_angles(positions, A_HEAD_DIM)
    cos_b, sin_b = rope_angles(positions, B_ROPE)
    for l in range(DEPTH):
        x = hybrid_layer(x, cos_a, sin_a, cos_b, sin_b,
                         g_mix_pre[l], g_mix_post[l], g_mlp_pre[l], g_mlp_post[l],
                         w_in[l], b_gate[l], sinks[l], q_norm[l], kv_norm[l],
                         w_uq[l], w_ukv[l], w_oa[l], w_ob[l], w_out[l],
                         w_mlp_in[l], w_mlp_out[l])
    return x


_drawn_inputs = setup_inputs


def setup_inputs(seed=0):
    import zlib

    import numpy as np

    out = dict(_drawn_inputs(seed))
    spreads = {}
    factors = {'sinks': 8.0}
    for name, (base, spread) in spreads.items():
        noise = np.random.default_rng([zlib.crc32(name.encode()), seed]).standard_normal(out[name].shape)
        drawn = base * np.exp(spread * noise) if base else spread * noise
        out[name] = __import__('jax').numpy.asarray(drawn.astype(out[name].dtype))
    for name, factor in factors.items():
        out[name] = (out[name] * factor).astype(out[name].dtype)
    return out
```

```python
from contextlib import ExitStack

import concourse.bass as bass
import numpy as np
from concourse import mybir

F32 = mybir.dt.float32
F32R = mybir.dt.float32r
I32 = mybir.dt.int32
BF16 = mybir.dt.bfloat16
ALU = mybir.AluOpType
ACT = mybir.ActivationFunctionType
AX = mybir.AxisListType.X

P = 128
D = 1024
SEQ = 256
DEPTH = 2
CHUNK = 64
TT = SEQ // P
KD = D // P
EPS = 1e-6
THETA = 10000.0
NEG = -1e30
AH, AKV, AD = 16, 2, 64
AG = AH // AKV
BH, BQL, BKL, BN, BR, BV = 8, 384, 256, 64, 32, 64
BQK = BN + BR
DFF = 4 * D
COL = 512
KQ, KV = BQL // P, BKL // P
C_Q, C_KV, C_CQ = 0, AH * AD, AH * AD + 2 * AKV * AD
C_CKV = C_CQ + BQL
C_GATE = C_CKV + BKL + BR
SCALE_A = AD ** -0.5
SCALE_B = BQK ** -0.5
NGAIN = KD + KD + KQ + KV
G_PRE, G_MLP, G_QN, G_KVN = 0, KD, 2 * KD, 2 * KD + KQ

LOADS = (
    [("cq", 4, BQL)] * 2 + [("ckv", 4, BKL + BR)] * 2 + [("kv", 4, 2 * AKV * AD)] * 2
    + [("q", 4, COL)] * 4 + [("uq", KQ, BQL)] * 2 + [("ukv", KV, COL)] * 2
    + [("gate", 4, COL)] * 8 + [("oa", 4, COL)] * 3 + [("ob", 4, COL)] + [("oa", 4, COL)] + [("ob", 4, COL)]
    + [("out", 4, COL)] * 4 + [("mlp", 4, COL)] * 32)
NL = len(LOADS)
NP = 2 * NL
RAW = 4
RING = 4
MJ = DFF // COL
L_MLP = 32
L_LOOP = L_MLP + 6
LOOP_J = MJ - 3
assert NL == 64 and LOADS[L_MLP][0] == "mlp" and LOADS[L_MLP - 1][0] == "out"


def piece_rows(p):
    nk = LOADS[p // 2][1]
    cut = (nk + 1) // 2
    return (0, cut) if p % 2 == 0 else (cut, nk)


QUANTA = ([("A", 0, g, h, 4) for g in range(AKV) for h in (0, 4)]
          + [("A", 1, g, h, 2) for g in range(AKV) for h in (0, 2, 4, 6)]
          + [("B", 0, 0, h, 4) for h in (0, 4)] + [("B", 1, 0, h, 2) for h in (0, 2, 4, 6)])
NQ = len(QUANTA)
NSTEP = NQ + 2
P_STEP = 28
YLAST = [1, 3, 7, 11, 13, 17]
NY = len(YLAST)
EXTRA = {1: [("qA", 1, 0)], 2: [("qA", 1, 1)],
         3: [("kB", 0, 0)], 4: [("qB", 0, 0)], 5: [("kB", 0, 1), ("y", 0)], 6: [("qB", 0, 1)],
         7: [("kB", 1, 0), ("y", 1)], 8: [("qB", 1, 0)], 9: [("kB", 1, 1)], 10: [("qB", 1, 1)],
         11: [("y", 2)], 15: [("y", 3)], 17: [("y", 4)]}


def fill_order():
    out = [("x", t, h) for t in range(TT) for h in range(2)]
    out += [("cq", 0), ("cq", 1), ("ckv",), ("kA",), ("qA", 0, 0), ("qA", 0, 1)]
    for i in range(NSTEP):
        if i >= 2:
            out.append(("P", i - 2))
        out += EXTRA.get(i, [])
    out += [("y", 5)] + [("mix", c, t) for c in range(2) for t in range(TT)]
    out += [("xm", t, h) for t in range(TT) for h in range(2)]
    out += [("h", j, t) for j in range(MJ) for t in range(TT)]
    return out


FILLS = fill_order()
NF = len(FILLS)
FILL = {name: i for i, name in enumerate(FILLS)}
HI_KINDS = ("x", "cq", "ckv", "y", "mix", "xm", "h")
HI_FILL = {name: i for i, name in enumerate(f for f in FILLS if f[0] in HI_KINDS)}
NHI = len(HI_FILL)
assert NF % 2 == 0

PROJ = {n: i for i, n in enumerate(("kv", "q0", "q1", "uq0", "uq1", "ukv0", "ukv1"))}
ROPED = {n: i for i, n in enumerate(("kA", "kpe", "q0", "q1", "qB"))}
GATED = {n: i for i, n in enumerate(("g0", "g1", "g2", "g3", "oa0", "ob0", "oa1", "ob1"))}
SUMS = {n: i for i, n in enumerate((s, t) for s in ("x", "cq", "ckv", "mixpost", "xm", "mlppost") for t in range(TT))}
NSUM = len(SUMS)


WIDTHS = (D, BQL, BKL)


class Pos:

    def __init__(self, l, j=None):
        self.l, self.j = l, j

    def count(self, per_layer, n, per_j=0):
        value = self.l * per_layer + n
        return value if self.j is None else value + self.j * per_j


class Steps:

    def __init__(self, eng, sem, per_layer=0, per_j=0):
        self.eng, self.sem, self.per_layer, self.per_j, self.n, self.pos = eng, sem, per_layer, per_j, 0, None

    def link(self, instruction):
        instruction.then_inc(self.sem, 1)
        self.n += 1
        self.eng.wait_ge(self.sem, self.n if self.pos is None else self.pos.count(self.per_layer, self.n, self.per_j))


def build(nc, x_d, pos_d, g_mix_pre, g_mix_post, g_mlp_pre, g_mlp_post, w_in, b_gate, sinks_d, q_norm,
          kv_norm, w_uq, w_ukv, w_oa, w_ob, w_out, w_mlp_in, w_mlp_out, out_d):
    ctx = ExitStack()
    with ctx:
        def sb(name, shape, dt=F32):
            return ctx.enter_context(nc.sbuf_tensor(name, shape, dt))

        def sem(name):
            return ctx.enter_context(nc.semaphore(name))

        raw = sb("raw", [P, RAW, 4 * COL])
        w_hi = sb("w_hi", [P, RING, 2 * COL], F32R)
        w_lo = sb("w_lo", [P, RING, 2 * COL], F32R)
        s1_hi = sb("s1_hi", [P, KD, SEQ], F32R)
        s1_lo = sb("s1_lo", [P, KD, SEQ], F32R)
        s2_hi = sb("s2_hi", [P, KD, SEQ], F32R)
        s2_lo = sb("s2_lo", [P, KD, SEQ], F32R)
        x = sb("x", [P, TT, D])
        tok = sb("tok", [P, TT, D])
        gate_a = sb("gate_a", [P, TT, D])
        gate_b = sb("gate_b", [P, TT, D])
        k_b = sb("k_b", [P, TT, BH * BQK])
        latent = sb("latent", [P, TT, BQL + BKL + BR])
        kv_a = sb("kv_a", [P, TT, 2 * AKV * AD])
        v_tail = sb("v_tail", [CHUNK, AKV * AD])
        v_b = sb("v_b", [P, TT, BH * BV])
        qT_a = sb("qT_a", [P, AG, SEQ])
        kT_a = sb("kT_a", [P, SEQ])
        qT_b = sb("qT_b", [BQK, BH, SEQ])
        kT_b = sb("kT_b", [BQK, BH, SEQ])
        probs = sb("probs", [P, 2, COL])
        probsT = sb("probsT", [P, 2, COL])
        neg_m = sb("neg_m", [P, TT * (AH + BH)])
        row_max = sb("row_max", [P, TT * (AH + BH)])
        row_sum = sb("row_sum", [P, TT * (AH + BH)])
        sink_e = sb("sink_e", [P, TT * AH])
        denom = sb("denom", [P, TT * (AH + BH)])
        neg_sink = sb("neg_sink", [P, AH])
        sink_in = sb("sink_in", [P, AH])
        bias_g = sb("bias_g", [P, 2 * D])
        post_g = sb("post_g", [P, 2, D])
        squares = sb("squares", [P, 2, D], BF16)
        sums = sb("sums", [P, 2, NSUM])
        var = sb("var", [P, 2, NSUM])
        rstd = sb("rstd", [P, NSUM])
        norm_k = sb("norm_k", [P, 5, 1])
        gain_rows = sb("gain_rows", [DEPTH * NGAIN, P])
        gain_all = sb("gain_all", [P, DEPTH, NGAIN])
        gain = sb("gain", [P, NGAIN])
        ident = sb("ident", [P, P])
        chunk_of = sb("chunk_of", [P, P], F32R)
        mask = sb("mask", [P, 3, 2 * P], F32R)
        pos_i = sb("pos_i", [P, TT], I32)
        pos_f = sb("pos_f", [P, TT])
        freq = sb("freq", [P, AD // 2])
        ang = sb("ang", [P, TT, AD // 2])
        turns = sb("turns", [P, TT, AD // 2])
        cost = sb("cost", [P, TT, AD // 2])
        sint = sb("sint", [P, TT, 2, AD // 2])

        acc = [ctx.enter_context(nc.psum_tensor(f"acc{i}", [P, COL], F32)) for i in range(4)]
        sc = [ctx.enter_context(nc.psum_tensor(f"sc{i}", [P, COL], F32)) for i in range(2)]
        tp = [ctx.enter_context(nc.psum_tensor(f"tp{i}", [P, COL], F32)) for i in range(2)]

        raw_full = [sem(f"raw_full{i}") for i in range(RAW)]
        hi_ready = sem("hi_ready")
        lo_ready = sem("lo_ready")
        piece_used = sem("piece_used")
        tile0_done = sem("tile0_done")
        tp_full = sem("tp_full")
        tp_hi = sem("tp_hi")
        tp_done = sem("tp_done")
        x_loaded = sem("x_loaded")
        x_ready = sem("x_ready")
        sums_ready = sem("sums_ready")
        rstd_ready = sem("rstd_ready")
        latent_out = sem("latent_out")
        proj_out = sem("proj_out")
        roped = sem("roped")
        scores_ready = sem("scores_ready")
        neg_max = sem("neg_max")
        sink_arg = sem("sink_arg")
        sink_exp = sem("sink_exp")
        probs_ready = sem("probs_ready")
        pv_done = sem("pv_done")
        y_out = sem("y_out")
        gated_out = sem("gated_out")
        tanh_done = sem("tanh_done")
        mixed = sem("mixed")
        relu_done = sem("relu_done")
        h_ready = sem("h_ready")
        gains_loaded = sem("gains_loaded")
        gains_turned = sem("gains_turned")
        gains_now = sem("gains_now")
        params_loaded = sem("params_loaded")
        pos_loaded = sem("pos_loaded")
        consts_ready = sem("consts_ready")
        angles = sem("angles")
        sines = sem("sines")
        vec_step = sem("vec_step")
        pool_step = sem("pool_step")
        act_step = sem("act_step")
        stored = sem("stored")

        NCONST = 6 + AD // 2

        def raw_view(p):
            n, N = p // 2, LOADS[p // 2][2]
            k0, k1 = piece_rows(p)
            return raw[:, n % RAW, k0 * N:k1 * N]

        def split_view(buf, p):
            k0, k1 = piece_rows(p)
            return buf[:, p % RING, 0:(k1 - k0) * LOADS[p // 2][2]]

        def stationary(name):
            kind = name[0]
            if kind in ("x", "xm"):
                _, t, h = name
                return s1_hi, s1_lo, 4 * h, 4, t
            if kind == "cq":
                return s2_hi, s2_lo, 0, KQ, name[1]
            if kind == "y":
                yi = name[1]
                if yi < 4:
                    return s2_hi, s2_lo, 4 * (yi % 2), 4, yi // 2
                return s1_hi, s1_lo, 4, 4, yi - 4
            if kind == "mix":
                return s1_hi, s1_lo, 4 * name[1], 4, name[2]
            if kind == "h":
                return s2_hi, s2_lo, 4 if name[1] == MJ - 1 else 0, 4, name[2]

        def bank(name):
            return tp[FILL[name] % 2]

        def q_col(i):
            kind, t, g, h, n = QUANTA[i]
            return t * AH + g * AG + h if kind == "A" else TT * AH + t * BH + h

        def q_of_group(t, g):
            return tok[:, t, :].rearrange("p (h g d) -> p g h d", g=AKV, h=AG)[:, g, :, :]

        def y_cols(yi):
            c = 8 * yi
            return slice(c, c + 8)

        def quantum_shape(i):
            kind, t, g, h, n = QUANTA[i]
            return n, COL // n, (CHUNK if kind == "A" and t == 1 else 0)

        def first_of_y(i):
            return next(y for y in range(NY) if i <= YLAST[y])

        block = ctx.enter_context(nc.Block())

        @block.sync
        def _(sp):
            sp.dma_start(x[:, 0, :], x_d[0, 0:P, :]).then_inc(x_loaded, 16)
            sp.dma_start(x[:, 1, :], x_d[0, P:2 * P, :]).then_inc(x_loaded, 16)

            def raw_free(pos, n):
                sp.wait_ge(lo_ready, pos.count(NP, 2 * n + 2, 8))

            def load(pos, n, src, wait=True):
                _, nk, N = LOADS[n]
                if wait:
                    raw_free(pos, n)
                sp.dma_start(raw[:, n % RAW, 0:nk * N].rearrange("p (k n) -> p k n", k=nk),
                             src.rearrange("(k p) n -> p k n", p=P)).then_inc(raw_full[n % RAW], 16)

            with sp.Fori(0, DEPTH) as l:
                pos = Pos(l)
                w = w_in[l]
                n = 0
                for c0, N in ((C_CQ, BQL), (C_CKV, BKL + BR), (C_KV, 2 * AKV * AD), (0, COL), (COL, COL)):
                    for h in range(2):
                        if n == 6:
                            raw_free(pos, n)
                            for src, dst in ((b_gate[l].rearrange("a d -> (a d)"), bias_g[:, :]),
                                             (g_mix_post[l], post_g[:, 0, :]), (g_mlp_post[l], post_g[:, 1, :]),
                                             (sinks_d[l], sink_in[:, :])):
                                sp.dma_start(dst, src.partition_broadcast(P)).then_inc(params_loaded, 16)
                        load(pos, n, w[h * COL:(h + 1) * COL, c0:c0 + N], wait=n != 6)
                        n += 1
                for c in range(2):
                    load(pos, n, w_uq[l][:, c * BQL:(c + 1) * BQL])
                    n += 1
                for c in range(2):
                    load(pos, n, w_ukv[l][:, c * COL:(c + 1) * COL])
                    n += 1
                for c in range(4):
                    for h in range(2):
                        load(pos, n, w[h * COL:(h + 1) * COL, C_GATE + c * COL:C_GATE + (c + 1) * COL])
                        n += 1
                for src, h, c in ((w_oa, 0, 0), (w_oa, 1, 0), (w_oa, 0, 1), (w_ob, 0, 0), (w_oa, 1, 1), (w_ob, 0, 1),
                                  (w_out, 0, 0), (w_out, 0, 1), (w_out, 1, 0), (w_out, 1, 1)):
                    load(pos, n, src[l][h * COL:(h + 1) * COL, c * COL:(c + 1) * COL])
                    n += 1
                assert n == L_MLP

                def mlp_in(pos, n, j):
                    for h in range(2):
                        load(pos, n + h, w_mlp_in[l][h * COL:(h + 1) * COL, bass.ts(j, COL)])

                def mlp_out(pos, n, j):
                    for c in range(2):
                        load(pos, n + c, w_mlp_out[l][bass.ts(j, COL), c * COL:(c + 1) * COL])

                mlp_in(pos, n, 0)
                mlp_in(pos, n + 2, 1)
                mlp_out(pos, n + 4, 0)
                with sp.Fori(0, LOOP_J) as j:
                    here = Pos(l, j)
                    mlp_in(here, L_LOOP, j + 2)
                    mlp_out(here, L_LOOP + 2, j + 1)
                n = L_LOOP + 4 * LOOP_J
                mlp_in(pos, n, MJ - 1)
                mlp_out(pos, n + 2, MJ - 2)
                mlp_out(pos, n + 4, MJ - 1)
                assert n + 6 == NL
            sp.wait_ge(x_ready, 2 * TT * DEPTH + TT)
            sp.dma_start(out_d[0].rearrange("(t p) d -> p t d", p=P), x[:, :, :]).then_inc(stored, 16)
            sp.wait_ge(stored, 16)

        @block.gpsimd
        def _(pool):
            g = nc.gpsimd
            steps = Steps(pool, pool_step)

            def const(ins):
                ins.then_inc(consts_ready, 1)

            steps.link(g.memset(ident[:, :], 0.0))
            const(g.affine_select(out=ident[:, :], in_=ident[:, :], compare_op=ALU.not_equal, fill=1.0,
                                  base=0, pattern=[[-1, P]], channel_multiplier=1))
            for i, value in enumerate([1.0 / w for w in WIDTHS] + [EPS, -0.5]):
                const(g.memset(norm_k[:, i], value))
            sel, mk = chunk_of[:, :].bitcast(F32), mask[:, :, :].bitcast(F32)
            steps.link(g.memset(sel, 0.0))
            steps.link(g.memset(mk, 0.0))
            for half in range(2):
                r = 2 * 32 * half
                steps.link(g.memset(sel[r:r + 1, 0:CHUNK], 1.0))
                steps.link(g.memset(sel[r + 32:r + 33, CHUNK:P], 1.0))
                steps.link(g.memset(mk[r:r + 1, 0, CHUNK:P], NEG))
                steps.link(g.memset(mk[r:r + 1, 1:3, P + CHUNK:2 * P], NEG))
                steps.link(g.memset(mk[r + 32:r + 33, 1, CHUNK:P], NEG))
            inv = np.float32(THETA) ** (-np.arange(0, AD, 2, dtype=np.float32) / np.float32(AD))
            for i in range(AD // 2):
                const(g.memset(freq[:, i:i + 1], float(inv[i])))

            def to_rstd(pos, name, width, parts=1):
                c = SUMS[name]
                pool.wait_ge(sums_ready, pos.count(NSUM, c + 1))
                if parts == 2:
                    steps.link(g.tensor_tensor(var[:, 0, c:c + 1], sums[:, 0, c:c + 1], sums[:, 1, c:c + 1], ALU.add))
                src = var if parts == 2 else sums
                steps.link(g.tensor_tensor(var[:, 1, c:c + 1], src[:, 0, c:c + 1], norm_k[:, WIDTHS.index(width)], ALU.mult))
                steps.link(g.tensor_tensor(var[:, 1, c:c + 1], var[:, 1, c:c + 1], norm_k[:, 3], ALU.add))
                g.tensor_tensor(rstd[:, c:c + 1], var[:, 1, c:c + 1], norm_k[:, 4], ALU.pow).then_inc(rstd_ready, 1)

            def square(pos, j, per_j=0):
                for t in range(TT):
                    pool.wait_ge(relu_done, pos.count(TT * MJ, TT * j + t + 1, TT))
                    g.tensor_tensor(tok[:, t, 0:COL], k_b[:, t, 0:COL], k_b[:, t, 0:COL], ALU.mult).then_inc(h_ready, 1)

            origin = steps.n
            with pool.Fori(0, DEPTH) as l:
                pos = Pos(l)
                steps.per_layer = 28
                steps.pos, first = pos, steps.n
                for t in range(TT):
                    to_rstd(pos, ("x", t), D)
                for t in range(TT):
                    to_rstd(pos, ("cq", t), BQL)
                for t in range(TT):
                    to_rstd(pos, ("ckv", t), BKL)
                for c in range(2):
                    cols = slice(c * COL, (c + 1) * COL)
                    for t in range(TT):
                        pool.wait_ge(gated_out, pos.count(16, 2 * GATED[f"ob{c}"] + t + 1))
                        g.tensor_tensor(tok[:, t, cols], gate_a[:, t, cols], gate_b[:, t, cols], ALU.add)\
                            .then_inc(mixed, 1)
                for t in range(TT):
                    to_rstd(pos, ("mixpost", t), D, parts=2)
                for t in range(TT):
                    to_rstd(pos, ("xm", t), D)
                square(pos, 0)
                square(pos, 1)
                with pool.Fori(0, LOOP_J) as j:
                    square(Pos(l, j), 2)
                square(pos, MJ - 1)
                for t in range(TT):
                    to_rstd(pos, ("mlppost", t), D, parts=2)
                assert steps.n - first == steps.per_layer, steps.n - first

        @block.scalar
        def _(act):
            s = nc.scalar
            steps = Steps(act, act_step)
            rows = ((g_mix_pre, G_PRE, KD), (g_mlp_pre, G_MLP, KD), (q_norm, G_QN, KQ), (kv_norm, G_KVN, KV))
            act.dma_start(pos_i[:, :], pos_d[0].rearrange("(t p) -> p t", p=P),
                          allow_slow_non_contiguous=True).then_inc(pos_loaded, 16)
            for l in range(DEPTH):
                for src, c, n in rows:
                    act.dma_start(gain_rows[l * NGAIN + c:l * NGAIN + c + n, :],
                                  src[l].rearrange("(k p) -> k p", p=P)).then_inc(gains_loaded, 16)

            act.wait_ge(angles, 1)
            s.activation(sint[:, :, 1, :], ang[:, :, :], ACT.Sin).then_inc(sines, 1)
            s.activation(turns[:, :, :], ang[:, :, :], ACT.Sin, scale=0.5).then_inc(sines, 1)

            def hi(pos, upto):
                while state[0] <= upto:
                    p = state[0]
                    n = p // 2
                    if p % 2 == 0:
                        act.wait_ge(raw_full[n % RAW], pos.count(16 * NL // RAW, 16 * (n // RAW + 1), 16))
                    act.wait_ge(piece_used, pos.count(NP, p + 1, 8))
                    s.copy(split_view(w_hi, p), raw_view(p)).then_inc(hi_ready, 1)
                    state[0] += 1

            def turned_hi(pos, name, per_j=0):
                act.wait_ge(tp_full, pos.count(NF, FILL[name] + 1, 2))
                b, kind = bank(name), name[0]
                if kind == "ckv":
                    for t in range(TT):
                        for k in range(KV):
                            i = 2 * t + k
                            ins = s.activation(s2_hi[:, KQ + k, t * P:(t + 1) * P], b[:, i * P:(i + 1) * P], ACT.Copy,
                                               scale=gain[:, G_KVN + k:G_KVN + k + 1])
                    ins.then_inc(tp_hi, 1)
                    return
                h, _, k0, nk, t = stationary(name)
                dst = h[:, k0:k0 + nk, t * P:(t + 1) * P]
                src = b[:, 0:nk * P].rearrange("p (k n) -> p k n", k=nk)
                col = {"x": G_PRE + k0, "xm": G_MLP + k0, "cq": G_QN}.get(kind)
                if col is None:
                    s.activation(dst, src, ACT.Copy, scale=0.5 if kind == "mix" else 1.0).then_inc(tp_hi, 1)
                    return
                for k in range(nk):
                    ins = s.activation(dst[:, k, :], src[:, k, :], ACT.Copy, scale=gain[:, col + k:col + k + 1])
                ins.then_inc(tp_hi, 1)

            def sum_squares(name, part, src):
                c = SUMS[name]
                return s.activation(squares[:, name[1], part * COL:part * COL + src.free_size()], src, ACT.Square,
                                    accum_out=sums[:, part, c:c + 1])

            def sum_x(pos, name, at):
                act.wait_ge(x_ready, pos.count(2 * TT, at))
                sum_squares(name, 0, x[:, name[1], :]).then_inc(sums_ready, 1)

            def rs(name):
                c = SUMS[name]
                return rstd[:, c:c + 1]

            def wait_rstd(pos, name):
                act.wait_ge(rstd_ready, pos.count(NSUM, SUMS[name] + 1))

            def used(pos, p, per_j=8):
                act.wait_ge(piece_used, pos.count(NP, RING + p + 1, per_j))

            def post_sums(pos, name):
                t = name[1]
                sum_squares(name, 0, acc[t][:, :])
                sum_squares(name, 1, acc[2 + t][:, :]).then_inc(sums_ready, 1)

            def relu(pos, j, p, banks):
                used(pos, p)
                for t in range(TT):
                    if j > 0:
                        act.wait_ge(h_ready, pos.count(TT * MJ, TT * (j - 1) + t + 1, TT))
                    s.activation(k_b[:, t, 0:COL], banks[t][:, :], ACT.Relu, scale=rs(("xm", t))).then_inc(relu_done, 1)

            def exps(pos, i):
                kind, t, g, h, n = QUANTA[i]
                n, w, skip = quantum_shape(i)
                c = q_col(i)
                act.wait_ge(neg_max, pos.count(NQ, i + 1))
                if i >= 2:
                    act.wait_ge(tp_full, pos.count(NF, FILL[("P", i - 2)] + 1))
                for a in range(n):
                    ins = s.activation(probs[:, i % 2, a * w + skip:(a + 1) * w], sc[i % 2][:, a * w + skip:(a + 1) * w],
                                       ACT.Exp, bias=neg_m[:, c + a:c + a + 1], scale=SCALE_A if kind == "A" else SCALE_B,
                                       accum_out=row_sum[:, c + a:c + a + 1])
                ins.then_inc(probs_ready, 1)

            state = [0]
            with act.Fori(0, DEPTH) as l:
                pos = Pos(l)
                state[0] = 0
                hi(pos, 0)
                act.wait_ge(gains_now, pos.count(1, 1))
                turned_hi(pos, ("x", 0, 0))
                hi(pos, 1)
                turned_hi(pos, ("x", 0, 1))
                hi(pos, 3)
                turned_hi(pos, ("x", 1, 0))
                turned_hi(pos, ("x", 1, 1))
                for t in range(TT):
                    sum_x(pos, ("x", t), t + 1)
                hi(pos, 6)
                for t in range(TT):
                    act.wait_ge(latent_out, pos.count(2 * TT, t + 1))
                    sum_squares(("cq", t), 0, latent[:, t, 0:BQL]).then_inc(sums_ready, 1)
                hi(pos, 10)
                for t in range(TT):
                    act.wait_ge(latent_out, pos.count(2 * TT, TT + t + 1))
                    sum_squares(("ckv", t), 0, latent[:, t, BQL:BQL + BKL]).then_inc(sums_ready, 1)
                hi(pos, 14)
                used(pos, 11)
                for t in range(TT):
                    if t == 0:
                        s.activation(v_tail[:, :], acc[0][CHUNK:P, AKV * AD:2 * AKV * AD], ACT.Copy,
                                     scale=rstd[CHUNK:P, SUMS[("x", 0)]:SUMS[("x", 0)] + 1])
                    s.activation(kv_a[:, t, :], acc[t][:, 0:2 * AKV * AD], ACT.Copy, scale=rs(("x", t))).then_inc(proj_out, 1)
                turned_hi(pos, ("cq", 0))
                turned_hi(pos, ("cq", 1))
                for c, p in ((0, 15), (1, 19)):
                    hi(pos, p + 3)
                    used(pos, p)
                    for t in range(TT):
                        s.activation(q_of_group(t, c), acc[2 * (1 - c) + t][:, :].rearrange("p (h d) -> p h d", h=AG), ACT.Copy,
                                     scale=rs(("x", t))).then_inc(proj_out, 1)
                    if c == 0:
                        turned_hi(pos, ("ckv",))
                for t in range(TT):
                    wait_rstd(pos, ("ckv", t))
                for c, p in ((0, 21), (1, 23)):
                    hi(pos, p + 3)
                    used(pos, p)
                    for t in range(TT):
                        s.activation(gate_b[:, t, c * BQL:(c + 1) * BQL], acc[2 * (1 - c) + t][:, 0:BQL], ACT.Copy,
                                     scale=rs(("cq", t))).then_inc(proj_out, 1)
                for c, p in ((0, 25), (1, 27)):
                    hi(pos, p + 3)
                    used(pos, p)
                    for t in range(TT):
                        src = acc[2 * (1 - c) + t][:, :].rearrange("p (h d) -> p h d", h=BH // 2)
                        kd = k_b[:, t, :].rearrange("p (h d) -> p h d", h=BH)[:, 4 * c:4 * c + 4, 0:BN]
                        vd = v_b[:, t, :].rearrange("p (h d) -> p h d", h=BH)[:, 4 * c:4 * c + 4, :]
                        s.activation(kd, src[:, :, 0:BN], ACT.Copy, scale=rs(("ckv", t)))
                        s.activation(vd, src[:, :, BN:BN + BV], ACT.Copy, scale=rs(("ckv", t))).then_inc(proj_out, 1)
                for i in range(NSTEP):
                    for name in EXTRA.get(i - 1, []):
                        if name[0] == "y":
                            turned_hi(pos, name)
                    if i % 4 == 0 and 0 < i <= 16:
                        c = i // 4 - 1
                        gt = gate_a if c < 2 else gate_b
                        for t in range(TT):
                            act.wait_ge(gated_out, pos.count(16, 2 * c + t + 1))
                            v = gt[:, t, (c % 2) * COL:(c % 2 + 1) * COL]
                            s.activation(v, v, ACT.Tanh, scale=0.5).then_inc(tanh_done, 1)
                    if i < NQ:
                        exps(pos, i)
                        if i in YLAST[:4]:
                            yi = YLAST.index(i)
                            act.wait_ge(sink_arg, pos.count(4, yi + 1))
                            s.activation(sink_e[:, y_cols(yi)], sink_e[:, y_cols(yi)], ACT.Exp).then_inc(sink_exp, 1)
                    hi(pos, P_STEP + 3 + i)
                p = P_STEP + NSTEP
                hi(pos, p + 4)
                turned_hi(pos, ("y", 5))
                hi(pos, 55 + 1)
                turned_hi(pos, ("mix", 0, 0))
                turned_hi(pos, ("mix", 0, 1))
                hi(pos, 57 + 3)
                turned_hi(pos, ("mix", 1, 0))
                turned_hi(pos, ("mix", 1, 1))
                hi(pos, 63)
                act.wait_ge(tile0_done, pos.count(2, 1))
                post_sums(pos, ("mixpost", 0))
                hi(pos, 65)
                used(pos, 63)
                post_sums(pos, ("mixpost", 1))
                turned_hi(pos, ("xm", 0, 0))
                turned_hi(pos, ("xm", 0, 1))
                hi(pos, 67)
                turned_hi(pos, ("xm", 1, 0))
                turned_hi(pos, ("xm", 1, 1))
                for t in range(TT):
                    sum_x(pos, ("xm", t), TT + t + 1)
                hi(pos, 70)
                for t in range(TT):
                    wait_rstd(pos, ("xm", t))
                relu(pos, 0, 67, acc)
                hi(pos, 72)
                for t in range(TT):
                    turned_hi(pos, ("h", 0, t))
                hi(pos, 74)
                relu(pos, 1, 71, sc)
                hi(pos, 79)
                base = 2 * L_LOOP
                assert base == 76
                with act.Fori(0, LOOP_J) as j:
                    here = Pos(l, j)
                    hi(here, base + 4)
                    for t in range(TT):
                        turned_hi(here, ("h", 1, t))
                    hi(here, base + 6)
                    relu(here, 2, base + 3, sc)
                    hi(here, base + 11)
                base += 8 * LOOP_J
                state[0] = base + 4
                hi(pos, base + 4)
                for t in range(TT):
                    turned_hi(pos, ("h", MJ - 2, t))
                hi(pos, base + 6)
                relu(pos, MJ - 1, base + 3, sc)
                hi(pos, base + 8)
                for t in range(TT):
                    turned_hi(pos, ("h", MJ - 1, t))
                hi(pos, NP - 1)
                act.wait_ge(tile0_done, pos.count(2, 2))
                post_sums(pos, ("mlppost", 0))
                used(pos, NP - 1)
                post_sums(pos, ("mlppost", 1))

        @block.vector
        def _(dve):
            v = nc.vector
            steps = Steps(dve, vec_step)

            dve.sem_inc(lo_ready, 2 * RAW)
            dve.sem_inc(tp_done, 2)
            dve.wait_ge(x_loaded, 16 * TT)
            dve.sem_inc(x_ready, TT)
            dve.wait_ge(consts_ready, NCONST)

            dve.wait_ge(gains_turned, 1)
            steps.link(v.tensor_copy(gain_all[:, :, :].rearrange("p l g -> p (l g)"), sc[0][:, 0:DEPTH * NGAIN]))

            dve.wait_ge(pos_loaded, 16)
            steps.link(v.tensor_copy(pos_f[:, :], pos_i[:, :]))
            for t in range(TT):
                steps.link(v.tensor_scalar(ang[:, t, :], freq[:, :], pos_f[:, t:t + 1], None, ALU.mult))
            magic = 1.5 * 2.0 ** 23
            two_pi = 2 * np.pi
            c1 = 6.28125
            c2 = float(np.floor((two_pi - c1) * 2 ** 20) / 2 ** 20)
            c3 = float(two_pi - c1 - c2)
            pi_in = 3.14159250259
            steps.link(v.tensor_scalar(turns[:, :, :], ang[:, :, :], 1.0 / two_pi, magic, ALU.mult, ALU.add))
            steps.link(v.tensor_scalar(turns[:, :, :], turns[:, :, :], magic, None, ALU.subtract))
            for c in (c1, c2, c3):
                steps.link(v.scalar_tensor_tensor(out=ang[:, :, :], in0=turns[:, :, :], scalar=-c, in1=ang[:, :, :],
                                                  op0=ALU.mult, op1=ALU.add))
            v.tensor_scalar(ang[:, :, :], ang[:, :, :], pi_in, -pi_in, ALU.min, ALU.max).then_inc(angles, 1)
            dve.wait_ge(sines, 2)
            steps.link(v.tensor_tensor(cost[:, :, :], turns[:, :, :], turns[:, :, :], ALU.mult))
            steps.link(v.tensor_scalar(cost[:, :, :], cost[:, :, :], -2.0, 1.0, ALU.mult, ALU.add))
            steps.link(v.tensor_scalar(sint[:, :, 0, :], sint[:, :, 1, :], -1.0, None, ALU.mult))

            def lo(pos, upto):
                while state[0] <= upto:
                    p = state[0]
                    dve.wait_ge(hi_ready, pos.count(NP, p + 1, 8))
                    v.tensor_tensor(split_view(w_lo, p), raw_view(p), split_view(w_hi, p).bitcast(F32), ALU.subtract)\
                        .then_inc(lo_ready, 1)
                    state[0] += 1

            def turned_lo(pos, name):
                dve.wait_ge(tp_hi, pos.count(NHI, HI_FILL[name] + 1, 2))
                b, kind = bank(name), name[0]
                if kind == "ckv":
                    for t in range(TT):
                        for k in range(KV):
                            i = 2 * t + k
                            ins = v.scalar_tensor_tensor(
                                out=s2_lo[:, KQ + k, t * P:(t + 1) * P], in0=b[:, i * P:(i + 1) * P],
                                scalar=gain[:, G_KVN + k:G_KVN + k + 1],
                                in1=s2_hi[:, KQ + k, t * P:(t + 1) * P].bitcast(F32), op0=ALU.mult, op1=ALU.subtract)
                    ins.then_inc(tp_done, 1)
                    return
                h, low, k0, nk, t = stationary(name)
                dst = low[:, k0:k0 + nk, t * P:(t + 1) * P]
                hiv = h[:, k0:k0 + nk, t * P:(t + 1) * P].bitcast(F32)
                src = b[:, 0:nk * P].rearrange("p (k n) -> p k n", k=nk)
                col = {"x": G_PRE + k0, "xm": G_MLP + k0, "cq": G_QN}.get(kind)
                if kind == "mix":
                    v.scalar_tensor_tensor(out=dst, in0=src, scalar=0.5, in1=hiv, op0=ALU.mult,
                                           op1=ALU.subtract).then_inc(tp_done, 1)
                elif col is None:
                    v.tensor_tensor(dst, src, hiv, ALU.subtract).then_inc(tp_done, 1)
                else:
                    for k in range(nk):
                        ins = v.scalar_tensor_tensor(out=dst[:, k, :], in0=src[:, k, :],
                                                     scalar=gain[:, col + k:col + k + 1], in1=hiv[:, k, :],
                                                     op0=ALU.mult, op1=ALU.subtract)
                    ins.then_inc(tp_done, 1)

            def turned_copy(pos, name):
                dve.wait_ge(tp_full, pos.count(NF, FILL[name] + 1))
                b = bank(name)
                if name[0] == "kA":
                    ins = v.tensor_copy(kT_a[:, :], b[:, 0:SEQ])
                elif name[0] == "qA":
                    _, t, h = name
                    ins = v.tensor_copy(qT_a[:, 4 * h:4 * h + 4, t * P:(t + 1) * P],
                                        b[:, :].rearrange("p (h n) -> p h n", h=4))
                elif name[0] in ("qB", "kB"):
                    _, t, h = name
                    dst = qT_b if name[0] == "qB" else kT_b
                    ins = v.tensor_copy(dst[:, 4 * h:4 * h + 4, t * P:(t + 1) * P],
                                        b[0:BQK, :].rearrange("p (h n) -> p h n", h=4))
                else:
                    i = name[1]
                    if i >= 2:
                        dve.wait_ge(pv_done, pos.count(NQ, i - 1))
                    if quantum_shape(i)[2]:
                        v.tensor_copy(probsT[0:CHUNK, i % 2, 0:2 * P], b[0:CHUNK, 0:2 * P])
                        ins = v.tensor_copy(probsT[:, i % 2, 2 * P:4 * P], b[:, 2 * P:4 * P])
                    else:
                        ins = v.tensor_copy(probsT[:, i % 2, :], b[:, :])
                ins.then_inc(tp_done, 1)

            def turned(pos, name):
                turned_lo(pos, name) if name[0] in HI_KINDS else turned_copy(pos, name)

            def used(pos, p):
                dve.wait_ge(piece_used, pos.count(NP, RING + p + 1))

            def rs(name):
                c = SUMS[name]
                return rstd[:, c:c + 1]

            def wait_rstd(pos, name):
                dve.wait_ge(rstd_ready, pos.count(NSUM, SUMS[name] + 1))

            def rope(q, heads, half, t, stride):
                n = 2 * heads * half
                tmp = probs[:, 0, 0:n].rearrange("p (h c d) -> p h c d", h=heads, c=2)
                sn = sint[:, t, :, ::stride].unsqueeze(1).to_broadcast([P, heads, 2, half])
                cs = cost[:, t, ::stride].unsqueeze(1).unsqueeze(1).to_broadcast([P, heads, 2, half])
                steps.link(v.tensor_tensor(tmp, q[:, :, ::-1, :], sn, ALU.mult))
                steps.link(v.tensor_tensor(q, q, cs, ALU.mult))
                return v.tensor_tensor(q, q, tmp, ALU.add)

            def row_maxima(pos, i):
                kind, t, g, h, n = QUANTA[i]
                n, w, skip = quantum_shape(i)
                c = q_col(i)
                dve.wait_ge(scores_ready, pos.count(NQ, i + 1))
                steps.link(v.tensor_reduce(row_max[:, c:c + n],
                                           sc[i % 2][:, :].rearrange("p (h k) -> p h k", h=n)[:, :, skip:w], AX, ALU.max))
                if kind == "A":
                    v.scalar_tensor_tensor(out=neg_m[:, c:c + n], in0=row_max[:, c:c + n], scalar=-SCALE_A,
                                           in1=neg_sink[:, g * AG + h:g * AG + h + n], op0=ALU.mult,
                                           op1=ALU.min).then_inc(neg_max, 1)
                else:
                    v.tensor_scalar(neg_m[:, c:c + n], row_max[:, c:c + n], -SCALE_B, None, ALU.mult).then_inc(neg_max, 1)
                if i in YLAST[:4]:
                    yi = YLAST.index(i)
                    g = yi % 2
                    dve.wait_ge(neg_max, pos.count(NQ, i + 1))
                    v.tensor_tensor(sink_e[:, y_cols(yi)], neg_m[:, y_cols(yi)], neg_sink[:, g * AG:(g + 1) * AG],
                                    ALU.subtract).then_inc(sink_arg, 1)

            def normalise(pos, yi):
                c = y_cols(yi)
                dve.wait_ge(probs_ready, pos.count(NQ, YLAST[yi] + 1))
                if yi < 4:
                    dve.wait_ge(sink_exp, pos.count(4, yi + 1))
                    steps.link(v.tensor_tensor(denom[:, c], row_sum[:, c], sink_e[:, c], ALU.add))
                    steps.link(v.reciprocal(denom[:, c], denom[:, c]))
                    t, g = yi // 2, yi % 2
                    dst = tok[:, t, g * COL:(g + 1) * COL]
                else:
                    steps.link(v.reciprocal(denom[:, c], row_sum[:, c]))
                    dst = latent[:, yi - 4, 0:COL]
                dve.wait_ge(pv_done, pos.count(NQ, YLAST[yi] + 1))
                v.tensor_tensor(dst.rearrange("p (h d) -> p h d", h=8),
                                acc[2 + yi % 2][:, :].rearrange("p (h d) -> p h d", h=8),
                                denom[:, c].unsqueeze(2).to_broadcast([P, 8, 64]), ALU.mult).then_inc(y_out, 1)

            def gate_logits(pos, c):
                used(pos, P_STEP + 4 * c + 3)
                gt = gate_a if c < 2 else gate_b
                for t in range(TT):
                    v.scalar_tensor_tensor(out=gt[:, t, (c % 2) * COL:(c % 2 + 1) * COL], in0=acc[t][:, :],
                                           scalar=rs(("x", t)), in1=bias_g[:, c * COL:(c + 1) * COL],
                                           op0=ALU.mult, op1=ALU.add).then_inc(gated_out, 1)

            def gated(pos, p, gt, c, banks):
                used(pos, p)
                for t in range(TT):
                    view = gt[:, t, c * COL:(c + 1) * COL]
                    v.scalar_tensor_tensor(out=view, in0=view, scalar=1.0, in1=banks[t][:, :], op0=ALU.add,
                                           op1=ALU.mult).then_inc(gated_out, 1)

            def update_x(pos, name, which):
                t = name[1]
                wait_rstd(pos, name)
                for c in range(2):
                    ins = v.scalar_tensor_tensor(out=probs[:, c, :], in0=acc[2 * c + t][:, :], scalar=rs(name),
                                                 in1=post_g[:, which, c * COL:(c + 1) * COL], op0=ALU.mult, op1=ALU.mult)
                steps.link(ins)
                v.tensor_tensor(x[:, t, :], x[:, t, :], probs[:, :, :].rearrange("p a b -> p (a b)"), ALU.add)\
                    .then_inc(x_ready, 1)
                dve.wait_ge(x_ready, pos.count(2 * TT, TT + TT * which + t + 1))

            state = [0]
            with dve.Fori(0, DEPTH) as l:
                pos = Pos(l)
                state[0] = 0
                steps.pos, first = pos, steps.n
                steps.per_layer = 54
                v.tensor_copy(gain[:, :], gain_all[:, l, :]).then_inc(gains_now, 1)
                dve.wait_ge(gains_now, pos.count(1, 1))
                lo(pos, 0)
                turned(pos, ("x", 0, 0))
                lo(pos, 1)
                turned(pos, ("x", 0, 1))
                lo(pos, 3)
                turned(pos, ("x", 1, 0))
                turned(pos, ("x", 1, 1))
                for n0, (c0, N, pair, p) in enumerate(((0, BQL, 0, 3), (BQL, BKL + BR, 1, 7))):
                    lo(pos, p + 3)
                    if n0 == 0:
                        for t in range(TT):
                            wait_rstd(pos, ("x", t))
                    used(pos, p)
                    for t in range(TT):
                        v.tensor_scalar(latent[:, t, c0:c0 + N], acc[2 * pair + t][:, 0:N], rs(("x", t)), None,
                                        ALU.mult).then_inc(latent_out, 1)
                lo(pos, 14)
                turned(pos, ("cq", 0))
                turned(pos, ("cq", 1))
                for t in range(TT):
                    dve.wait_ge(proj_out, pos.count(14, 2 * PROJ["kv"] + t + 1))
                    rope(kv_a[:, t, 0:AKV * AD].rearrange("p (h c d) -> p h c d", h=AKV, c=2), AKV, AD // 2, t, 1)\
                        .then_inc(roped, 1)
                    dve.wait_ge(roped, pos.count(10, t + 1))
                for t in range(TT):
                    kp = latent[:, t, BQL + BKL:BQL + BKL + BR]
                    steps.link(rope(kp.rearrange("p (h c d) -> p h c d", h=1, c=2), 1, BR // 2, t, 2))
                    v.tensor_copy(k_b[:, t, :].rearrange("p (h d) -> p h d", h=BH)[:, :, BN:BQK],
                                  kp.unsqueeze(1).to_broadcast([P, BH, BR])).then_inc(roped, 1)
                lo(pos, 18)
                turned(pos, ("ckv",))
                for c, p in ((0, 18), (1, 22)):
                    lo(pos, p)
                    for t in range(TT):
                        dve.wait_ge(proj_out, pos.count(14, 2 * PROJ[f"q{c}"] + t + 1))
                        rope(q_of_group(t, c).rearrange("p h (c d) -> p h c d", c=2), AG, AD // 2, t, 1)\
                            .then_inc(roped, 1)
                        dve.wait_ge(roped, pos.count(10, 2 * ROPED[f"q{c}"] + t + 1))
                lo(pos, 26)
                for t in range(TT):
                    dve.wait_ge(proj_out, pos.count(14, 2 * PROJ["uq1"] + t + 1))
                    qb = gate_b[:, t, 0:BH * BQK].rearrange("p (h d) -> p h d", h=BH)[:, :, BN:BQK]
                    rope(qb.rearrange("p h (c d) -> p h c d", c=2), BH, BR // 2, t, 2).then_inc(roped, 1)
                    dve.wait_ge(roped, pos.count(10, 2 * ROPED["qB"] + t + 1))
                dve.wait_ge(params_loaded, pos.count(64, 64))
                v.tensor_scalar(neg_sink[:, :], sink_in[:, :], -1.0, None, ALU.mult)
                lo(pos, 30)
                turned(pos, ("kA",))
                turned(pos, ("qA", 0, 0))
                turned(pos, ("qA", 0, 1))
                for i in range(NSTEP):
                    if i % 4 == 0 and 0 < i <= 16:
                        gate_logits(pos, i // 4 - 1)
                    for name in EXTRA.get(i - 1, []):
                        turned(pos, name)
                    if i - 3 in YLAST:
                        normalise(pos, YLAST.index(i - 3))
                    if i < NQ:
                        row_maxima(pos, i)
                    if i >= 2:
                        turned(pos, ("P", i - 2))
                    lo(pos, P_STEP + 3 + i)
                p = P_STEP + NSTEP
                dve.wait_ge(tanh_done, pos.count(4 * TT, 4 * TT))
                gated(pos, p - 1, gate_a, 0, acc[0:2])
                normalise(pos, 5)
                lo(pos, p + 4)
                turned(pos, ("y", 5))
                lo(pos, 53 + 1)
                gated(pos, 51, gate_b, 0, acc[0:2])
                lo(pos, 55 + 1)
                turned(pos, ("mix", 0, 0))
                turned(pos, ("mix", 0, 1))
                gated(pos, 53, gate_a, 1, sc)
                gated(pos, 55, gate_b, 1, acc[2:4])
                lo(pos, 57 + 3)
                turned(pos, ("mix", 1, 0))
                turned(pos, ("mix", 1, 1))
                lo(pos, 63)
                update_x(pos, ("mixpost", 0), 0)
                lo(pos, 65)
                turned(pos, ("xm", 0, 0))
                turned(pos, ("xm", 0, 1))
                lo(pos, 66)
                update_x(pos, ("mixpost", 1), 0)
                lo(pos, 67)
                turned(pos, ("xm", 1, 0))
                turned(pos, ("xm", 1, 1))
                lo(pos, 72)
                for t in range(TT):
                    turned(pos, ("h", 0, t))
                lo(pos, 79)
                base = 2 * L_LOOP
                with dve.Fori(0, LOOP_J) as j:
                    here = Pos(l, j)
                    lo(here, base + 4)
                    for t in range(TT):
                        turned(here, ("h", 1, t))
                    lo(here, base + 11)
                base += 8 * LOOP_J
                state[0] = base + 4
                lo(pos, base + 4)
                for t in range(TT):
                    turned(pos, ("h", MJ - 2, t))
                lo(pos, base + 8)
                for t in range(TT):
                    turned(pos, ("h", MJ - 1, t))
                lo(pos, NP - 1)
                update_x(pos, ("mlppost", 0), 1)
                update_x(pos, ("mlppost", 1), 1)
                assert steps.n - first == steps.per_layer, steps.n - first

        @block.tensor
        def _(pe):
            mm = nc.tensor.matmul
            pe.sem_inc(piece_used, RING)
            pe.wait_ge(consts_ready, NCONST)
            pe.wait_ge(gains_loaded, 16 * 4 * DEPTH)
            n = DEPTH * NGAIN
            nc.tensor.transpose(sc[0][:, 0:n], gain_rows[:, :], ident[0:n, 0:n]).then_inc(gains_turned, 1)

            def turn(pos, name, blocks, per_j=0):
                b = bank(name)
                pe.wait_ge(tp_done, pos.count(NF, FILL[name] + 1, 2))
                for i, src in reversed(list(enumerate(blocks))):
                    rows = src.free_size()
                    ins = nc.tensor.transpose(b[0:rows, i * P:(i + 1) * P], src, ident[:, :])
                ins.then_inc(tp_full, 1)

            def turned(pos, name, per_j=0):
                pe.wait_ge(tp_done, pos.count(NF, 2 + FILL[name] + 1, 2))

            def product(pos, p, k0, stat, banks, start=False, stop=False, tiles=(0, 1), release=True, mark=None):
                a, b = piece_rows(p)
                N = LOADS[p // 2][2]
                h, low = stat
                pe.wait_ge(lo_ready, pos.count(NP, 2 * RAW + p + 1, 8))
                wh = split_view(w_hi, p).rearrange("p (k n) -> p k n", k=b - a)
                wl = split_view(w_lo, p).rearrange("p (k n) -> p k n", k=b - a)
                for t in tiles:
                    tk = slice(t * P, (t + 1) * P)
                    for k in range(b - a):
                        kk = k0 + a + k
                        mm(banks[t][:, 0:N], h[:, kk, tk], wh[:, k, :], start=(start and k == 0), stop=False)
                        mm(banks[t][:, 0:N], h[:, kk, tk], wl[:, k, :], start=False, stop=False)
                        ins = mm(banks[t][:, 0:N], low[:, kk, tk], wh[:, k, :], start=False,
                                 stop=(stop and k == b - a - 1))
                if release:
                    ins.then_inc(piece_used, 1)
                elif mark is not None:
                    ins.then_inc(mark, 1)

            s1, s2 = (s1_hi, s1_lo), (s2_hi, s2_lo)

            def turn_x(pos, kind, t):
                pe.wait_ge(x_ready, pos.count(2 * TT, (TT if kind == "xm" else 0) + t + 1))
                for h in range(2):
                    turn(pos, (kind, t, h), [x[:, t, (4 * h + k) * P:(4 * h + k + 1) * P] for k in range(4)])

            def turn_h(pos, j, at):
                for t in range(TT):
                    pe.wait_ge(h_ready, pos.count(TT * MJ, TT * j + t + 1, TT))
                    turn(pos, ("h", at, t), [tok[:, t, k * P:(k + 1) * P] for k in range(4)])

            def scores(pos, i):
                kind, t, g, h, n = QUANTA[i]
                n, w, skip = quantum_shape(i)
                if i >= 2:
                    pe.wait_ge(probs_ready, pos.count(NQ, i - 1))
                r0, r1 = (64 * g, 64 * g + 64) if kind == "A" else (0, P)
                which = 0 if t == 0 else (1 if kind == "A" else 2)
                b = sc[i % 2]
                view = b[:, :].rearrange("p (h k) -> p h k", h=n)[:, :, skip:w]
                mk = mask[r0:r1, which, skip:w].unsqueeze(1).to_broadcast([r1 - r0, n, w - skip])
                mm(view, chunk_of[r0:r1, :], mk, start=True, stop=False)
                for a in range(n):
                    if kind == "A":
                        q = qT_a[r0:r1, h + a, t * P:(t + 1) * P]
                        k = kT_a[r0:r1, skip:w]
                    else:
                        q = qT_b[:, h + a, t * P:(t + 1) * P]
                        k = kT_b[:, h + a, 0:w]
                    ins = mm(b[:, a * w + skip:(a + 1) * w], q, k, start=False, stop=(a == n - 1))
                ins.then_inc(scores_ready, 1)

            def turn_probs(pos, i):
                n, w, skip = quantum_shape(i)
                pe.wait_ge(probs_ready, pos.count(NQ, i + 1))
                blocks = []
                for b in range(w // P):
                    for a in range(n):
                        blocks.append(probs[:, i % 2, a * w + b * P + (skip if b == 0 else 0):a * w + (b + 1) * P])
                turn(pos, ("P", i), blocks)

            def values(pos, i):
                kind, t, g, h, n = QUANTA[i]
                n, w, skip = quantum_shape(i)
                yi = first_of_y(i)
                turned(pos, ("P", i))
                if i == 0 or i - 1 in YLAST:
                    if yi >= 2:
                        pe.wait_ge(y_out, pos.count(NY, yi - 1))
                y = acc[2 + yi % 2]
                for a in range(n):
                    for b in range(w // P):
                        rows = CHUNK if (skip and b == 0) else P
                        pt = probsT[0:rows, i % 2, (b * n + a) * P:(b * n + a + 1) * P]
                        if kind == "A":
                            vv = v_tail[:, g * AD:(g + 1) * AD] if rows == CHUNK else \
                                kv_a[:, b, (AKV + g) * AD:(AKV + g + 1) * AD]
                        else:
                            vv = v_b[:, b, (h + a) * BV:(h + a + 1) * BV]
                        ins = mm(y[:, (h + a) * 64:(h + a + 1) * 64], pt, vv, start=(b == 0), stop=(b == w // P - 1))
                ins.then_inc(pv_done, 1)

            def extra(pos, name):
                if name[0] == "qA":
                    _, t, h = name
                    blocks = [tok[:, t, (4 * h + a) * AKV * AD:(4 * h + a + 1) * AKV * AD] for a in range(4)]
                elif name[0] in ("qB", "kB"):
                    _, t, h = name
                    src = gate_b if name[0] == "qB" else k_b
                    blocks = [src[:, t, (4 * h + a) * BQK:(4 * h + a + 1) * BQK] for a in range(4)]
                else:
                    yi = name[1]
                    pe.wait_ge(y_out, pos.count(NY, yi + 1))
                    src = tok[:, yi // 2, (yi % 2) * COL:(yi % 2 + 1) * COL] if yi < 4 else latent[:, yi - 4, 0:COL]
                    blocks = [src[:, k * P:(k + 1) * P] for k in range(4)]
                turn(pos, name, blocks)

            def projected(pos, name):
                pe.wait_ge(proj_out, pos.count(14, 2 * PROJ[name] + 2))

            def gate_free(pos, name):
                pe.wait_ge(gated_out, pos.count(16, 2 * GATED[name] + 2))

            pair = [acc[0:2], acc[2:4]]
            with pe.Fori(0, DEPTH) as l:
                pos = Pos(l)
                turn_x(pos, "x", 0)
                turned(pos, ("x", 0, 1))
                for p in range(4):
                    product(pos, p, 4 * (p // 2), s1, pair[0], p == 0, p == 3, tiles=(0,), release=False)
                turn_x(pos, "x", 1)
                turned(pos, ("x", 1, 1))
                for p in range(4):
                    product(pos, p, 4 * (p // 2), s1, pair[0], p == 0, p == 3, tiles=(1,))
                for i, p in enumerate(range(4, 8)):
                    product(pos, p, 4 * (i // 2), s1, pair[1], i == 0, i == 3)
                pe.wait_ge(latent_out, pos.count(2 * TT, TT))
                for i, p in enumerate(range(8, 12)):
                    product(pos, p, 4 * (i // 2), s1, pair[0], i == 0, i == 3)
                for t in range(TT):
                    turn(pos, ("cq", t), [latent[:, t, k * P:(k + 1) * P] for k in range(KQ)])
                pe.wait_ge(latent_out, pos.count(2 * TT, 2 * TT))
                for i, p in enumerate(range(12, 16)):
                    product(pos, p, 4 * (i // 2), s1, pair[1], i == 0, i == 3)
                turn(pos, ("ckv",), [latent[:, t, BQL + k * P:BQL + (k + 1) * P] for t in range(TT) for k in range(KV)])
                projected(pos, "kv")
                for i, p in enumerate(range(16, 20)):
                    product(pos, p, 4 * (i // 2), s1, pair[0], i == 0, i == 3)
                turned(pos, ("ckv",))
                for c, (q, before, k0) in enumerate((("uq0", "q0", 0), ("uq1", "q1", 0), ("ukv0", "uq0", KQ), ("ukv1", "uq1", KQ))):
                    projected(pos, before)
                    for i in range(2):
                        product(pos, 20 + 2 * c + i, k0, s2, pair[1 - c % 2], i == 0, i == 1)
                pe.wait_ge(roped, pos.count(10, 2 * ROPED["kA"] + 2))
                turn(pos, ("kA",), [kv_a[:, t, 0:AKV * AD] for t in range(TT)])
                pe.wait_ge(roped, pos.count(10, 2 * ROPED["q1"] + 2))
                extra(pos, ("qA", 0, 0))
                extra(pos, ("qA", 0, 1))
                turned(pos, ("qA", 0, 1))
                projected(pos, "ukv1")
                for i in range(NSTEP):
                    if i < NQ:
                        scores(pos, i)
                    if i >= 2:
                        turn_probs(pos, i - 2)
                    p = P_STEP + i
                    if i % 4 == 0 and i > 0:
                        gate_free(pos, f"g{i // 4 - 1}")
                    if i < 16:
                        product(pos, p, 4 * (i % 4 // 2), s1, pair[0], i % 4 == 0, i % 4 == 3)
                    else:
                        if i == 16:
                            turned(pos, ("y", 3))
                        product(pos, p, 4 * (i % 4 // 2), s2, pair[0], i % 4 == 0, i % 4 == 3)
                    if i >= 2:
                        values(pos, i - 2)
                    for name in EXTRA.get(i, []):
                        if i == 3:
                            pe.wait_ge(roped, pos.count(10, 2 * ROPED["qB"] + 2))
                        extra(pos, name)
                product(pos, 48, 0, s2, sc, True, False)
                extra(pos, ("y", 5))
                product(pos, 49, 0, s2, sc)
                gate_free(pos, "oa0")
                turned(pos, ("y", 5))
                product(pos, 50, 4, s1, pair[0], True, False)
                product(pos, 51, 4, s1, pair[0], False, True)
                product(pos, 52, 4, s2, sc)
                product(pos, 53, 4, s2, sc, False, True)
                for t in range(TT):
                    pe.wait_ge(mixed, pos.count(4, t + 1))
                    turn(pos, ("mix", 0, t), [tok[:, t, k * P:(k + 1) * P] for k in range(4)])
                product(pos, 54, 4, s1, pair[1], True, False)
                product(pos, 55, 4, s1, pair[1], False, True)
                turned(pos, ("mix", 0, 1))
                product(pos, 56, 0, s1, pair[0], True)
                product(pos, 57, 0, s1, pair[0])
                for t in range(TT):
                    pe.wait_ge(mixed, pos.count(4, 2 + t + 1))
                    turn(pos, ("mix", 1, t), [tok[:, t, COL + k * P:COL + (k + 1) * P] for k in range(4)])
                product(pos, 58, 0, s1, pair[1], True)
                product(pos, 59, 0, s1, pair[1])
                turned(pos, ("mix", 1, 1))

                def finish(pos, p, k0, stat):
                    for t in range(TT):
                        for i in range(4):
                            product(pos, p + i, k0, stat, pair[i // 2], False, i % 2 == 1, tiles=(t,), release=(t == 1),
                                    mark=tile0_done if i == 3 else None)

                finish(pos, 60, 4, s1)

                def mlp_in(pos, p, banks, j, at):
                    for i in range(4):
                        if i == 2:
                            turn_h(pos, j, at)
                        product(pos, p + i, 4 * (i // 2), s1, banks, i == 0, i == 3)

                def mlp_out(pos, p, start=False):
                    for i in range(4):
                        product(pos, p + i, 0, s2, pair[i // 2], start and i % 2 == 0)

                turn_x(pos, "xm", 0)
                turned(pos, ("xm", 0, 1))
                for p in range(64, 68):
                    product(pos, p, 4 * (p // 2 % 2), s1, pair[0], p == 64, p == 67, tiles=(0,), release=False)
                turn_x(pos, "xm", 1)
                turned(pos, ("xm", 1, 1))
                for p in range(64, 68):
                    product(pos, p, 4 * (p // 2 % 2), s1, pair[0], p == 64, p == 67, tiles=(1,))
                mlp_in(pos, 68, sc, 0, 0)
                turned(pos, ("h", 0, 1))
                mlp_out(pos, 72, start=True)
                with pe.Fori(0, LOOP_J) as j:
                    here = Pos(l, j)
                    pe.wait_ge(relu_done, here.count(TT * MJ, 2 * TT, TT))
                    mlp_in(here, 76, sc, 1, 1)
                    turned(here, ("h", 1, 1))
                    mlp_out(here, 80)
                base = 2 * L_LOOP + 8 * LOOP_J
                pe.wait_ge(relu_done, pos.count(TT * MJ, TT * (MJ - 1)))
                mlp_in(pos, base, sc, MJ - 2, MJ - 2)
                turned(pos, ("h", MJ - 2, 1))
                product(pos, base + 4, 0, s2, pair[0])
                product(pos, base + 5, 0, s2, pair[0])
                turn_h(pos, MJ - 1, MJ - 1)
                product(pos, base + 6, 0, s2, pair[1])
                product(pos, base + 7, 0, s2, pair[1])
                turned(pos, ("h", MJ - 1, 1))
                finish(pos, base + 8, 4, s2)


_INS = ["x", "positions", "g_mix_pre", "g_mix_post", "g_mlp_pre", "g_mlp_post", "w_in", "b_gate", "sinks",
        "q_norm", "kv_norm", "w_uq", "w_ukv", "w_oa", "w_ob", "w_out", "w_mlp_in", "w_mlp_out"]


def kernel(**inputs):
    import concourse.bacc as bacc
    from concourse.bass_utils import run_bass_kernel_spmd

    nc = bacc.Bacc("TRN2", target_bir_lowering=False, num_devices=1)
    arrays, args = {}, []
    for name in _INS:
        a = np.ascontiguousarray(inputs[name])
        arrays["in_" + name] = a
        args.append(nc.dram_tensor("in_" + name, a.shape, mybir.dt.from_np(a.dtype), kind="ExternalInput").ap())
    out = nc.dram_tensor("out_x", (1, SEQ, D), F32, kind="ExternalOutput").ap()
    build(nc, *args, out)
    result = run_bass_kernel_spmd(nc, [arrays], core_ids=[0])
    return result.results[0]["out_x"]
```

```python
from contextlib import ExitStack

import concourse.bass as bass
import numpy as np
from concourse import mybir

F32 = mybir.dt.float32
F32R = mybir.dt.float32r
I32 = mybir.dt.int32
BF16 = mybir.dt.bfloat16
ALU = mybir.AluOpType
ACT = mybir.ActivationFunctionType
AX = mybir.AxisListType.X

P = 128
D = 1024
SEQ = 256
DEPTH = 2
CHUNK = 64
TT = SEQ // P
KD = D // P
EPS = 1e-6
THETA = 10000.0
NEG = -1e30
AH, AKV, AD = 16, 2, 64
AG = AH // AKV
BH, BQL, BKL, BN, BR, BV = 8, 384, 256, 64, 32, 64
BQK = BN + BR
DFF = 4 * D
COL = 512
KQ, KV = BQL // P, BKL // P
C_Q, C_KV, C_CQ = 0, AH * AD, AH * AD + 2 * AKV * AD
C_CKV = C_CQ + BQL
C_GATE = C_CKV + BKL + BR
SCALE_A = AD ** -0.5
SCALE_B = BQK ** -0.5
NGAIN = KD + KD + KQ + KV
G_PRE, G_MLP, G_QN, G_KVN = 0, KD, 2 * KD, 2 * KD + KQ
GAINS = ((G_PRE, KD), (G_MLP, KD), (G_QN, KQ), (G_KVN, KV))

LOADS = (
    [("cq", 4, BQL)] * 2 + [("ckv", 4, BKL + BR)] * 2 + [("kv", 4, 2 * AKV * AD)] * 2
    + [("q", 4, COL)] * 4 + [("uq", KQ, BQL)] * 2 + [("ukv", KV, COL)] * 2
    + [("gate", 4, COL)] * 8 + [("oa", 4, COL)] * 3 + [("ob", 4, COL)] + [("oa", 4, COL)] + [("ob", 4, COL)]
    + [("out", 4, COL)] * 4 + [("mlp", 4, COL)] * 32)
NL = len(LOADS)
NP = 2 * NL
RAW = 4
RING = 4
MJ = DFF // COL
L_MLP = 32
L_LOOP = L_MLP + 6
LOOP_J = MJ - 3
assert NL == 64 and LOADS[L_MLP][0] == "mlp" and LOADS[L_MLP - 1][0] == "out"


def piece_rows(p):
    nk = LOADS[p // 2][1]
    cut = (nk + 1) // 2
    return (0, cut) if p % 2 == 0 else (cut, nk)


QUANTA = ([("A", 0, g, h, 4) for g in range(AKV) for h in (0, 4)]
          + [("A", 1, g, h, 2) for g in range(AKV) for h in (0, 2, 4, 6)]
          + [("B", 0, 0, h, 4) for h in (0, 4)] + [("B", 1, 0, h, 2) for h in (0, 2, 4, 6)])
NQ = len(QUANTA)
NSTEP = NQ + 2
P_STEP = 28
YLAST = [1, 3, 7, 11, 13, 17]
NY = len(YLAST)
EXTRA = {1: [("qA", 1, 0)], 2: [("qA", 1, 1)],
         3: [("kB", 0, 0)], 4: [("qB", 0, 0)], 5: [("kB", 0, 1), ("y", 0)], 6: [("qB", 0, 1)],
         7: [("kB", 1, 0), ("y", 1)], 8: [("qB", 1, 0)], 9: [("kB", 1, 1)], 10: [("qB", 1, 1)],
         11: [("y", 2)], 15: [("y", 3)], 17: [("y", 4)]}


def fill_order():
    out = [("x", t, h) for t in range(TT) for h in range(2)]
    out += [("cq", 0), ("cq", 1), ("ckv",), ("kA",), ("qA", 0, 0), ("qA", 0, 1)]
    for i in range(NSTEP):
        if i >= 2:
            out.append(("P", i - 2))
        out += EXTRA.get(i, [])
    out += [("y", 5)] + [("mix", c, t) for c in range(2) for t in range(TT)]
    out += [("xm", t, h) for t in range(TT) for h in range(2)]
    out += [("h", j, t) for j in range(MJ) for t in range(TT)]
    return out


FILLS = fill_order()
NF = len(FILLS)
FILL = {name: i for i, name in enumerate(FILLS)}
HI_KINDS = ("x", "cq", "ckv", "y", "mix", "xm", "h")
HI_FILL = {name: i for i, name in enumerate(f for f in FILLS if f[0] in HI_KINDS)}
NHI = len(HI_FILL)
assert NF % 2 == 0

PROJ = {n: i for i, n in enumerate(("kv", "q0", "q1", "uq0", "uq1", "ukv0", "ukv1"))}
POOL_ROPED = {n: i for i, n in enumerate(("kA", "kpe", "q", "qB"))}
GATED = {n: i for i, n in enumerate(("g0", "g1", "g2", "g3", "oa0", "ob0", "oa1", "ob1"))}
SUMS = {n: i for i, n in enumerate((s, t) for s in ("x", "cq", "ckv", "mixpost", "xm", "mlppost") for t in range(TT))}
NSUM = len(SUMS)
SUM_PARTS = [(n, h) for n in SUMS for h in range(2 if n[0] in ("mixpost", "mlppost") else 1)]
NPART = len(SUM_PARTS)
WIDTH = {"x": D, "cq": BQL, "ckv": BKL, "mixpost": D, "xm": D, "mlppost": D}


class Pos:

    def __init__(self, l, j=None):
        self.l, self.j = l, j

    def count(self, per_layer, n, per_j=0):
        value = self.l * per_layer + n
        return value if self.j is None else value + self.j * per_j


class Steps:

    def __init__(self, eng, sem, per_layer=0, per_j=0):
        self.eng, self.sem, self.per_layer, self.per_j, self.n, self.pos = eng, sem, per_layer, per_j, 0, None

    def link(self, instruction):
        instruction.then_inc(self.sem, 1)
        self.n += 1
        self.eng.wait_ge(self.sem, self.n if self.pos is None else self.pos.count(self.per_layer, self.n, self.per_j))


def build(nc, x_d, pos_d, g_mix_pre, g_mix_post, g_mlp_pre, g_mlp_post, w_in, b_gate, sinks_d, q_norm,
          kv_norm, w_uq, w_ukv, w_oa, w_ob, w_out, w_mlp_in, w_mlp_out, out_d):
    ctx = ExitStack()
    with ctx:
        def sb(name, shape, dt=F32):
            return ctx.enter_context(nc.sbuf_tensor(name, shape, dt))

        def sem(name):
            return ctx.enter_context(nc.semaphore(name))

        raw = sb("raw", [P, RAW, 4 * COL])
        w_hi = sb("w_hi", [P, RING, 2 * COL], F32R)
        w_lo = sb("w_lo", [P, RING, 2 * COL], F32R)
        s1_hi = sb("s1_hi", [P, KD, SEQ], F32R)
        s1_lo = sb("s1_lo", [P, KD, SEQ], F32R)
        s2_hi = sb("s2_hi", [P, KD, SEQ], F32R)
        s2_lo = sb("s2_lo", [P, KD, SEQ], F32R)
        x = sb("x", [P, TT, D])
        tok = sb("tok", [P, TT, D])
        gate_a = sb("gate_a", [P, TT, D])
        gate_b = sb("gate_b", [P, TT, D])
        k_b = sb("k_b", [P, TT, BH * BQK])
        latent = sb("latent", [P, TT, BQL + BKL + BR])
        kv_a = sb("kv_a", [P, TT, 2 * AKV * AD])
        v_tail = sb("v_tail", [CHUNK, AKV * AD])
        v_b = sb("v_b", [P, TT, BH * BV])
        qT_a = sb("qT_a", [P, AG, SEQ])
        kT_a = sb("kT_a", [P, SEQ])
        qT_b = sb("qT_b", [BQK, BH, SEQ])
        kT_b = sb("kT_b", [BQK, BH, SEQ])
        probs = sb("probs", [P, 2, COL])
        probsT = sb("probsT", [P, 2, COL])
        neg_m = sb("neg_m", [P, TT * (AH + BH)])
        row_max = sb("row_max", [P, TT * (AH + BH)])
        row_sum = sb("row_sum", [P, TT * (AH + BH)])
        sink_e = sb("sink_e", [P, TT * AH])
        denom = sb("denom", [P, TT * (AH + BH)])
        neg_sink = sb("neg_sink", [P, AH])
        sink_in = sb("sink_in", [P, AH])
        bias_g = sb("bias_g", [P, 2 * D])
        post_g = sb("post_g", [P, 2, D])
        squares = sb("squares", [P, 2, D], BF16)
        sums = sb("sums", [P, 2, NSUM])
        var = sb("var", [P, NSUM])
        rstd = sb("rstd", [P, NSUM])
        norm_k = sb("norm_k", [P, 2, 1])
        gain_rows = sb("gain_rows", [DEPTH * NGAIN, P])
        gain_all = sb("gain_all", [P, DEPTH + 1, NGAIN])
        gain = sb("gain", [P, NGAIN])
        ident = sb("ident", [P, P])
        chunk_of = sb("chunk_of", [P, P], F32R)
        mask = sb("mask", [P, 3, 2 * P], F32R)
        pos_i = sb("pos_i", [P, TT], I32)
        pos_f = sb("pos_f", [P, TT])
        freq = sb("freq", [P, AD // 2])
        ang = sb("ang", [P, TT, AD // 2])
        turns = sb("turns", [P, TT, AD // 2])
        cost = sb("cost", [P, TT, AD // 2])
        sint = sb("sint", [P, TT, 2, AD // 2])

        acc = [ctx.enter_context(nc.psum_tensor(f"acc{i}", [P, COL], F32)) for i in range(4)]
        sc = [ctx.enter_context(nc.psum_tensor(f"sc{i}", [P, COL], F32)) for i in range(2)]
        tp = [ctx.enter_context(nc.psum_tensor(f"tp{i}", [P, COL], F32)) for i in range(2)]

        raw_full = [sem(f"raw_full{i}") for i in range(RAW)]
        hi_ready = sem("hi_ready")
        lo_ready = sem("lo_ready")
        piece_used = sem("piece_used")
        tile0_done = sem("tile0_done")
        tp_full = sem("tp_full")
        tp_hi = sem("tp_hi")
        tp_done = sem("tp_done")
        x_loaded = [sem(f"x_loaded{t}") for t in range(TT)]
        x_ready = [sem(f"x_ready{t}") for t in range(TT)]
        sums_ready = sem("sums_ready")
        rstd_ready = sem("rstd_ready")
        latent_out = sem("latent_out")
        proj_out = sem("proj_out")
        roped = sem("roped")
        pool_roped = sem("pool_roped")
        scores_ready = sem("scores_ready")
        neg_max = sem("neg_max")
        sink_arg = sem("sink_arg")
        sink_exp = sem("sink_exp")
        probs_ready = sem("probs_ready")
        pv_done = sem("pv_done")
        y_out = sem("y_out")
        gated_out = sem("gated_out")
        tanh_done = sem("tanh_done")
        mixed = sem("mixed")
        relu_done = sem("relu_done")
        h_ready = sem("h_ready")
        gains_loaded = sem("gains_loaded")
        gains_turned = sem("gains_turned")
        gains_now = sem("gains_now")
        sinks_loaded = sem("sinks_loaded")
        bias_loaded = sem("bias_loaded")
        post_loaded = sem("post_loaded")
        pos_loaded = sem("pos_loaded")
        ident_ready = sem("ident_ready")
        consts_ready = sem("consts_ready")
        tables_ready = sem("tables_ready")
        freq_ready = sem("freq_ready")
        angles = sem("angles")
        sines = sem("sines")
        vec_step = sem("vec_step")
        pool_step = sem("pool_step")
        act_step = sem("act_step")
        stored = [sem(f"stored{t}") for t in range(TT)]

        def raw_view(p):
            n, N = p // 2, LOADS[p // 2][2]
            k0, k1 = piece_rows(p)
            return raw[:, n % RAW, k0 * N:k1 * N]

        def split_view(buf, p):
            k0, k1 = piece_rows(p)
            return buf[:, p % RING, 0:(k1 - k0) * LOADS[p // 2][2]]

        def stationary(name):
            kind = name[0]
            if kind in ("x", "xm"):
                _, t, h = name
                return s1_hi, s1_lo, 4 * h, 4, t
            if kind == "cq":
                return s2_hi, s2_lo, 0, KQ, name[1]
            if kind == "y":
                yi = name[1]
                if yi < 4:
                    return s2_hi, s2_lo, 4 * (yi % 2), 4, yi // 2
                return s1_hi, s1_lo, 4, 4, yi - 4
            if kind == "mix":
                return s1_hi, s1_lo, 4 * name[1], 4, name[2]
            if kind == "h":
                return s2_hi, s2_lo, 4 if name[1] == MJ - 1 else 0, 4, name[2]

        def bank(name):
            return tp[FILL[name] % 2]

        def q_col(i):
            kind, t, g, h, n = QUANTA[i]
            return t * AH + g * AG + h if kind == "A" else TT * AH + t * BH + h

        def q_of_group(t, g):
            return tok[:, t, :].rearrange("p (h g d) -> p g h d", g=AKV, h=AG)[:, g, :, :]

        def y_cols(yi):
            c = 8 * yi
            return slice(c, c + 8)

        def quantum_shape(i):
            kind, t, g, h, n = QUANTA[i]
            return n, COL // n, (CHUNK if kind == "A" and t == 1 else 0)

        def first_of_y(i):
            return next(y for y in range(NY) if i <= YLAST[y])

        def rope(eng, steps, scratch, q, heads, half, t, stride, copies=None):
            n = 2 * heads * half
            tmp = scratch[:, 0:n].rearrange("p (h c d) -> p h c d", h=heads, c=2)
            sn = sint[:, t, :, ::stride].unsqueeze(1).to_broadcast([P, heads, 2, half])
            cs = cost[:, t, ::stride].unsqueeze(1).unsqueeze(1).to_broadcast([P, heads, 2, half])
            steps.link(eng.tensor_tensor(tmp, q[:, :, ::-1, :], sn, ALU.mult))
            steps.link(eng.tensor_tensor(q, q, cs, ALU.mult))
            if copies is None:
                return eng.tensor_tensor(q, q, tmp, ALU.add)
            a, b = (u.rearrange("p h c d -> p h (c d)").to_broadcast(list(copies.shape)) for u in (q, tmp))
            return eng.tensor_tensor(copies, a, b, ALU.add)

        block = ctx.enter_context(nc.Block())

        @block.sync
        def _(sp):
            sp.dma_start(pos_i[:, :], pos_d[0].rearrange("(t p) -> p t", p=P),
                         allow_slow_non_contiguous=True).then_inc(pos_loaded, 16)
            sp.dma_start(x[:, 0, :], x_d[0, 0:P, :]).then_inc(x_loaded[0], 16)
            for src, (c, n) in zip((g_mix_pre, g_mlp_pre, q_norm, kv_norm), GAINS):
                sp.dma_start(gain_rows[DEPTH * c:DEPTH * (c + n), :],
                             src.rearrange("l (k p) -> (l k) p", p=P)).then_inc(gains_loaded, 16)

            def raw_free(pos, n):
                sp.wait_ge(lo_ready, pos.count(NP, 2 * n + 2, 8))

            def load(pos, n, src, wait=True):
                _, nk, N = LOADS[n]
                if wait:
                    raw_free(pos, n)
                sp.dma_start(raw[:, n % RAW, 0:nk * N].rearrange("p (k n) -> p k n", k=nk),
                             src.rearrange("(k p) n -> p k n", p=P)).then_inc(raw_full[n % RAW], 16)

            with sp.Fori(0, DEPTH) as l:
                pos = Pos(l)
                w = w_in[l]
                n = 0
                for c0, N in ((C_CQ, BQL), (C_CKV, BKL + BR), (C_KV, 2 * AKV * AD), (0, COL), (COL, COL)):
                    for h in range(2):
                        if n == 6:
                            raw_free(pos, n)
                            sp.dma_start(sink_in[:, :], sinks_d[l].partition_broadcast(P)).then_inc(sinks_loaded, 16)
                        load(pos, n, w[h * COL:(h + 1) * COL, c0:c0 + N], wait=n != 6)
                        n += 1
                for c in range(2):
                    load(pos, n, w_uq[l][:, c * BQL:(c + 1) * BQL])
                    n += 1
                for c in range(2):
                    load(pos, n, w_ukv[l][:, c * COL:(c + 1) * COL])
                    n += 1
                sp.dma_start(bias_g[:, :], b_gate[l].rearrange("a d -> (a d)").partition_broadcast(P))\
                    .then_inc(bias_loaded, 16)
                for c in range(4):
                    if c == 3:
                        for i, src in enumerate((g_mix_post, g_mlp_post)):
                            sp.dma_start(post_g[:, i, :], src[l].partition_broadcast(P)).then_inc(post_loaded, 16)
                    for h in range(2):
                        load(pos, n, w[h * COL:(h + 1) * COL, C_GATE + c * COL:C_GATE + (c + 1) * COL])
                        n += 1
                for src, h, c in ((w_oa, 0, 0), (w_oa, 1, 0), (w_oa, 0, 1), (w_ob, 0, 0), (w_oa, 1, 1), (w_ob, 0, 1),
                                  (w_out, 0, 0), (w_out, 0, 1), (w_out, 1, 0), (w_out, 1, 1)):
                    load(pos, n, src[l][h * COL:(h + 1) * COL, c * COL:(c + 1) * COL])
                    n += 1
                assert n == L_MLP

                def mlp_in(pos, n, j):
                    for h in range(2):
                        load(pos, n + h, w_mlp_in[l][h * COL:(h + 1) * COL, bass.ts(j, COL)])

                def mlp_out(pos, n, j):
                    for c in range(2):
                        load(pos, n + c, w_mlp_out[l][bass.ts(j, COL), c * COL:(c + 1) * COL])

                mlp_in(pos, n, 0)
                mlp_in(pos, n + 2, 1)
                mlp_out(pos, n + 4, 0)
                with sp.Fori(0, LOOP_J) as j:
                    here = Pos(l, j)
                    mlp_in(here, L_LOOP, j + 2)
                    mlp_out(here, L_LOOP + 2, j + 1)
                n = L_LOOP + 4 * LOOP_J
                mlp_in(pos, n, MJ - 1)
                mlp_out(pos, n + 2, MJ - 2)
                mlp_out(pos, n + 4, MJ - 1)
                assert n + 6 == NL
            for t in range(TT):
                sp.wait_ge(x_ready[t], 2 + 4 * DEPTH)
                sp.dma_start(out_d[0, t * P:(t + 1) * P, :], x[:, t, :]).then_inc(stored[t], 16)
            for t in range(TT):
                sp.wait_ge(stored[t], 16)

        @block.gpsimd
        def _(pool):
            g = nc.gpsimd
            steps = Steps(pool, pool_step)

            inv = np.float32(THETA) ** (-np.arange(0, AD, 2, dtype=np.float32) / np.float32(AD))
            for i in range(AD // 2):
                ins = g.memset(freq[:, i:i + 1], float(inv[i]))
            ins.then_inc(freq_ready, 1)
            pool.wait_ge(freq_ready, 1)
            steps.link(g.memset(ident[:, :], 0.0))
            g.affine_select(out=ident[:, :], in_=ident[:, :], compare_op=ALU.not_equal, fill=1.0,
                            base=0, pattern=[[-1, P]], channel_multiplier=1).then_inc(ident_ready, 1)
            pool.wait_ge(ident_ready, 1)
            for i, value in enumerate([EPS, -0.5]):
                ins = g.memset(norm_k[:, i], value)
            steps.link(ins)

            sel, mk = chunk_of[:, :].bitcast(F32), mask[:, :, :].bitcast(F32)
            steps.link(g.memset(sel, 0.0))
            steps.link(g.memset(mk, 0.0))
            for half in range(2):
                r = 2 * 32 * half
                steps.link(g.memset(sel[r:r + 1, 0:CHUNK], 1.0))
                steps.link(g.memset(sel[r + 32:r + 33, CHUNK:P], 1.0))
                steps.link(g.memset(mk[r:r + 1, 0, CHUNK:P], NEG))
                steps.link(g.memset(mk[r:r + 1, 1:3, P + CHUNK:2 * P], NEG))
                g.memset(mk[r + 32:r + 33, 1, CHUNK:P], NEG).then_inc(consts_ready, 1)
                pool.wait_ge(consts_ready, half + 1)

            pool.wait_ge(sines, 2)
            steps.link(g.tensor_tensor(cost[:, :, :], turns[:, :, :], turns[:, :, :], ALU.mult))
            steps.link(g.tensor_scalar(cost[:, :, :], cost[:, :, :], -2.0, 1.0, ALU.mult, ALU.add))
            g.tensor_scalar(sint[:, :, 0, :], sint[:, :, 1, :], -1.0, None, ALU.mult).then_inc(tables_ready, 1)
            pool.wait_ge(tables_ready, 1)

            def to_rstd(pos, name):
                c = SUMS[name]
                v = var[:, c:c + 1]
                pool.wait_ge(sums_ready, pos.count(NPART, SUM_PARTS.index((name, 0)) + 1))
                steps.link(g.tensor_tensor(v, sums[:, 0, c:c + 1], norm_k[:, 0], ALU.add))
                if (name, 1) in SUM_PARTS:
                    pool.wait_ge(sums_ready, pos.count(NPART, SUM_PARTS.index((name, 1)) + 1))
                    steps.link(g.tensor_tensor(v, v, sums[:, 1, c:c + 1], ALU.add))
                g.tensor_tensor(rstd[:, c:c + 1], var[:, c:c + 1], norm_k[:, 1], ALU.pow).then_inc(rstd_ready, 1)

            def pool_rope(q, heads, half, t, stride, copies=None):
                return rope(g, steps, gate_a[:, 1, 0:COL], q, heads, half, t, stride, copies)

            def square(pos, j, per_j=0):
                for t in range(TT):
                    pool.wait_ge(relu_done, pos.count(TT * MJ, TT * j + t + 1, TT))
                    g.tensor_tensor(tok[:, t, 0:COL], k_b[:, t, 0:COL], k_b[:, t, 0:COL], ALU.mult).then_inc(h_ready, 1)

            origin = steps.n
            with pool.Fori(0, DEPTH) as l:
                pos = Pos(l)
                steps.per_layer = 32
                steps.pos, first = pos, steps.n
                for t in range(TT):
                    to_rstd(pos, ("x", t))
                for t in range(TT):
                    to_rstd(pos, ("cq", t))
                for t in range(TT):
                    to_rstd(pos, ("ckv", t))
                for t in range(TT):
                    pool.wait_ge(proj_out, pos.count(14, 2 * PROJ["kv"] + t + 1))
                    pool_rope(kv_a[:, t, 0:AKV * AD].rearrange("p (h c d) -> p h c d", h=AKV, c=2), AKV, AD // 2, t, 1)\
                        .then_inc(pool_roped, 1)
                    pool.wait_ge(pool_roped, pos.count(8, t + 1))
                for t in range(TT):
                    pool.wait_ge(latent_out, pos.count(2 * TT, TT + t + 1))
                    kp = latent[:, t, BQL + BKL:BQL + BKL + BR]
                    pool_rope(kp.rearrange("p (h c d) -> p h c d", h=1, c=2), 1, BR // 2, t, 2,
                              copies=k_b[:, t, :].rearrange("p (h d) -> p h d", h=BH)[:, :, BN:BQK])\
                        .then_inc(pool_roped, 1)
                    pool.wait_ge(pool_roped, pos.count(8, 2 * POOL_ROPED["kpe"] + t + 1))
                for c in range(2):
                    pool.wait_ge(proj_out, pos.count(14, 2 * PROJ[f"q{c}"] + 2))
                    pool_rope(q_of_group(1, c).rearrange("p h (c d) -> p h c d", c=2), AG, AD // 2, 1, 1)\
                        .then_inc(pool_roped, 1)
                    pool.wait_ge(pool_roped, pos.count(8, 2 * POOL_ROPED["q"] + c + 1))
                for t in range(TT):
                    pool.wait_ge(proj_out, pos.count(14, 2 * PROJ["uq1"] + t + 1))
                    qb = gate_b[:, t, 0:BH * BQK].rearrange("p (h d) -> p h d", h=BH)[:, :, BN:BQK]
                    pool_rope(qb.rearrange("p h (c d) -> p h c d", c=2), BH, BR // 2, t, 2).then_inc(pool_roped, 1)
                    pool.wait_ge(pool_roped, pos.count(8, 2 * POOL_ROPED["qB"] + t + 1))
                for c in range(2):
                    cols = slice(c * COL, (c + 1) * COL)
                    for t in range(TT):
                        pool.wait_ge(gated_out, pos.count(16, 2 * GATED[f"ob{c}"] + t + 1))
                        g.tensor_tensor(tok[:, t, cols], gate_a[:, t, cols], gate_b[:, t, cols], ALU.add)\
                            .then_inc(mixed, 1)
                for name in ("mixpost", "xm"):
                    for t in range(TT):
                        to_rstd(pos, (name, t))
                square(pos, 0)
                square(pos, 1)
                with pool.Fori(0, LOOP_J) as j:
                    square(Pos(l, j), 2)
                square(pos, MJ - 1)
                for t in range(TT):
                    to_rstd(pos, ("mlppost", t))
                assert steps.n - first == steps.per_layer, steps.n - first

        @block.scalar
        def _(act):
            s = nc.scalar
            steps = Steps(act, act_step)
            act.wait_ge(angles, 1)
            s.activation(sint[:, :, 1, :], ang[:, :, :], ACT.Sin).then_inc(sines, 1)
            s.activation(turns[:, :, :], ang[:, :, :], ACT.Sin, scale=0.5).then_inc(sines, 1)

            act.wait_ge(x_loaded[0], 16)
            act.dma_start(x[:, 1, :], x_d[0, P:2 * P, :]).then_inc(x_loaded[1], 16)

            act.wait_ge(sines, 2)
            s.activation(neg_m[:, 0:1], turns[:, 0, 0:1], ACT.Exp)

            def hi(pos, upto):
                while state[0] <= upto:
                    p = state[0]
                    n = p // 2
                    if p % 2 == 0:
                        act.wait_ge(raw_full[n % RAW], pos.count(16 * NL // RAW, 16 * (n // RAW + 1), 16))
                    act.wait_ge(piece_used, pos.count(NP, p + 1, 8))
                    s.copy(split_view(w_hi, p), raw_view(p)).then_inc(hi_ready, 1)
                    state[0] += 1

            def turned_hi(pos, name, per_j=0):
                act.wait_ge(tp_full, pos.count(NF, FILL[name] + 1, 2))
                b, kind = bank(name), name[0]
                if kind == "ckv":
                    for t in range(TT):
                        for k in range(KV):
                            i = 2 * t + k
                            ins = s.activation(s2_hi[:, KQ + k, t * P:(t + 1) * P], b[:, i * P:(i + 1) * P], ACT.Copy,
                                               scale=gain[:, G_KVN + k:G_KVN + k + 1])
                    ins.then_inc(tp_hi, 1)
                    return
                h, _, k0, nk, t = stationary(name)
                dst = h[:, k0:k0 + nk, t * P:(t + 1) * P]
                src = b[:, 0:nk * P].rearrange("p (k n) -> p k n", k=nk)
                col = {"x": G_PRE + k0, "xm": G_MLP + k0, "cq": G_QN}.get(kind)
                if col is None:
                    s.activation(dst, src, ACT.Copy, scale=0.5 if kind == "mix" else 1.0).then_inc(tp_hi, 1)
                    return
                for k in range(nk):
                    ins = s.activation(dst[:, k, :], src[:, k, :], ACT.Copy, scale=gain[:, col + k:col + k + 1])
                ins.then_inc(tp_hi, 1)

            def sum_squares(name, part, src):
                c = SUMS[name]
                return s.activation(squares[:, name[1], part * COL:part * COL + src.free_size()], src, ACT.Square,
                                    scale=WIDTH[name[0]] ** -0.5, accum_out=sums[:, part, c:c + 1])

            def sum_x(pos, name, at):
                act.wait_ge(x_loaded[name[1]], 16)
                act.wait_ge(x_ready[name[1]], pos.count(4, at))
                sum_squares(name, 0, x[:, name[1], :]).then_inc(sums_ready, 1)

            def rs(name):
                c = SUMS[name]
                return rstd[:, c:c + 1]

            def wait_rstd(pos, name):
                act.wait_ge(rstd_ready, pos.count(NSUM, SUMS[name] + 1))

            def used(pos, p, per_j=8):
                act.wait_ge(piece_used, pos.count(NP, RING + p + 1, per_j))

            def post_sums(pos, name, p, between=None):
                t = name[1]
                for c in range(2):
                    if t == 0:
                        act.wait_ge(tile0_done, pos.count(4, (0 if name[0] == "mixpost" else 2) + c + 1))
                    else:
                        used(pos, p - 2 + 2 * c)
                    sum_squares(name, c, acc[2 * c + t][:, :]).then_inc(sums_ready, 1)
                    if c == 0 and between is not None:
                        hi(pos, between)

            def relu(pos, j, p, banks):
                used(pos, p)
                for t in range(TT):
                    if j > 0:
                        act.wait_ge(h_ready, pos.count(TT * MJ, TT * (j - 1) + t + 1, TT))
                    s.activation(k_b[:, t, 0:COL], banks[t][:, :], ACT.Relu, scale=rs(("xm", t))).then_inc(relu_done, 1)

            def exps(pos, i):
                kind, t, g, h, n = QUANTA[i]
                n, w, skip = quantum_shape(i)
                c = q_col(i)
                act.wait_ge(neg_max, pos.count(NQ, i + 1))
                if i >= 2:
                    act.wait_ge(tp_full, pos.count(NF, FILL[("P", i - 2)] + 1))
                for a in range(n):
                    ins = s.activation(probs[:, i % 2, a * w + skip:(a + 1) * w], sc[i % 2][:, a * w + skip:(a + 1) * w],
                                       ACT.Exp, bias=neg_m[:, c + a:c + a + 1], scale=SCALE_A if kind == "A" else SCALE_B,
                                       accum_out=row_sum[:, c + a:c + a + 1])
                ins.then_inc(probs_ready, 1)

            state = [0]
            with act.Fori(0, DEPTH) as l:
                pos = Pos(l)
                state[0] = 0
                act.wait_ge(gains_now, pos.count(1, 1))
                turned_hi(pos, ("x", 0, 0))
                hi(pos, 0)
                turned_hi(pos, ("x", 0, 1))
                hi(pos, 3)
                turned_hi(pos, ("x", 1, 0))
                turned_hi(pos, ("x", 1, 1))
                for t in range(TT):
                    sum_x(pos, ("x", t), 2)
                hi(pos, 6)
                for t in range(TT):
                    act.wait_ge(latent_out, pos.count(2 * TT, t + 1))
                    sum_squares(("cq", t), 0, latent[:, t, 0:BQL]).then_inc(sums_ready, 1)
                hi(pos, 10)
                for t in range(TT):
                    act.wait_ge(latent_out, pos.count(2 * TT, TT + t + 1))
                    sum_squares(("ckv", t), 0, latent[:, t, BQL:BQL + BKL]).then_inc(sums_ready, 1)
                hi(pos, 14)
                used(pos, 11)
                for t in range(TT):
                    if t == 0:
                        s.activation(v_tail[:, :], acc[0][CHUNK:P, AKV * AD:2 * AKV * AD], ACT.Copy,
                                     scale=rstd[CHUNK:P, SUMS[("x", 0)]:SUMS[("x", 0)] + 1])
                    s.activation(kv_a[:, t, :], acc[t][:, 0:2 * AKV * AD], ACT.Copy, scale=rs(("x", t))).then_inc(proj_out, 1)
                turned_hi(pos, ("cq", 0))
                turned_hi(pos, ("cq", 1))
                for c, p in ((0, 15), (1, 19)):
                    hi(pos, p + 3)
                    used(pos, p)
                    for t in range(TT):
                        s.activation(q_of_group(t, c), acc[2 * (1 - c) + t][:, :].rearrange("p (h d) -> p h d", h=AG), ACT.Copy,
                                     scale=rs(("x", t))).then_inc(proj_out, 1)
                    if c == 0:
                        turned_hi(pos, ("ckv",))
                for t in range(TT):
                    wait_rstd(pos, ("ckv", t))
                for c, p in ((0, 21), (1, 23)):
                    hi(pos, p + 3)
                    used(pos, p)
                    for t in range(TT):
                        s.activation(gate_b[:, t, c * BQL:(c + 1) * BQL], acc[2 * (1 - c) + t][:, 0:BQL], ACT.Copy,
                                     scale=rs(("cq", t))).then_inc(proj_out, 1)
                for c, p in ((0, 25), (1, 27)):
                    hi(pos, p + 3)
                    used(pos, p)
                    for t in range(TT):
                        src = acc[2 * (1 - c) + t][:, :].rearrange("p (h d) -> p h d", h=BH // 2)
                        kd = k_b[:, t, :].rearrange("p (h d) -> p h d", h=BH)[:, 4 * c:4 * c + 4, 0:BN]
                        vd = v_b[:, t, :].rearrange("p (h d) -> p h d", h=BH)[:, 4 * c:4 * c + 4, :]
                        s.activation(kd, src[:, :, 0:BN], ACT.Copy, scale=rs(("ckv", t)))
                        s.activation(vd, src[:, :, BN:BN + BV], ACT.Copy, scale=rs(("ckv", t))).then_inc(proj_out, 1)
                for i in range(NSTEP):
                    for name in EXTRA.get(i - 1, []):
                        if name[0] == "y":
                            turned_hi(pos, name)
                    if i % 4 == 0 and 0 < i <= 16:
                        c = i // 4 - 1
                        gt = gate_a if c < 2 else gate_b
                        for t in range(TT):
                            act.wait_ge(gated_out, pos.count(16, 2 * c + t + 1))
                            v = gt[:, t, (c % 2) * COL:(c % 2 + 1) * COL]
                            s.activation(v, v, ACT.Tanh, scale=0.5).then_inc(tanh_done, 1)
                    if i < NQ:
                        exps(pos, i)
                        if i in YLAST[:4]:
                            yi = YLAST.index(i)
                            act.wait_ge(sink_arg, pos.count(4, yi + 1))
                            s.activation(sink_e[:, y_cols(yi)], sink_e[:, y_cols(yi)], ACT.Exp).then_inc(sink_exp, 1)
                    hi(pos, P_STEP + 3 + i)
                p = P_STEP + NSTEP
                hi(pos, p + 4)
                turned_hi(pos, ("y", 5))
                hi(pos, 55 + 1)
                turned_hi(pos, ("mix", 0, 0))
                turned_hi(pos, ("mix", 0, 1))
                hi(pos, 57 + 3)
                turned_hi(pos, ("mix", 1, 0))
                turned_hi(pos, ("mix", 1, 1))
                hi(pos, 63)
                post_sums(pos, ("mixpost", 0), 63)
                hi(pos, 65)
                post_sums(pos, ("mixpost", 1), 63, between=66)
                turned_hi(pos, ("xm", 0, 0))
                turned_hi(pos, ("xm", 0, 1))
                hi(pos, 67)
                turned_hi(pos, ("xm", 1, 0))
                turned_hi(pos, ("xm", 1, 1))
                for t in range(TT):
                    sum_x(pos, ("xm", t), 4)
                hi(pos, 70)
                for t in range(TT):
                    wait_rstd(pos, ("xm", t))
                relu(pos, 0, 67, acc)
                hi(pos, 72)
                for t in range(TT):
                    turned_hi(pos, ("h", 0, t))
                hi(pos, 74)
                relu(pos, 1, 71, sc)
                hi(pos, 79)
                base = 2 * L_LOOP
                assert base == 76
                with act.Fori(0, LOOP_J) as j:
                    here = Pos(l, j)
                    hi(here, base + 4)
                    for t in range(TT):
                        turned_hi(here, ("h", 1, t))
                    hi(here, base + 6)
                    relu(here, 2, base + 3, sc)
                    hi(here, base + 11)
                base += 8 * LOOP_J
                state[0] = base + 4
                hi(pos, base + 4)
                for t in range(TT):
                    turned_hi(pos, ("h", MJ - 2, t))
                hi(pos, base + 6)
                relu(pos, MJ - 1, base + 3, sc)
                hi(pos, base + 8)
                for t in range(TT):
                    turned_hi(pos, ("h", MJ - 1, t))
                hi(pos, NP - 1)
                post_sums(pos, ("mlppost", 0), NP - 1)
                post_sums(pos, ("mlppost", 1), NP - 1)

        @block.vector
        def _(dve):
            v = nc.vector
            steps = Steps(dve, vec_step)

            dve.sem_inc(lo_ready, 2 * RAW)
            dve.sem_inc(tp_done, 2)
            for t in range(TT):
                dve.sem_inc(x_ready[t], 2)
            dve.wait_ge(freq_ready, 1)
            dve.wait_ge(pos_loaded, 16)
            steps.link(v.tensor_copy(pos_f[:, :], pos_i[:, :]))
            for t in range(TT):
                ins = v.tensor_scalar(ang[:, t, :], freq[:, :], pos_f[:, t:t + 1], None, ALU.mult)
            steps.link(ins)
            magic = 1.5 * 2.0 ** 23
            two_pi = 2 * np.pi
            c1 = 6.28125
            c2 = float(np.floor((two_pi - c1) * 2 ** 20) / 2 ** 20)
            c3 = float(two_pi - c1 - c2)
            pi_in = 3.14159250259
            steps.link(v.tensor_scalar(turns[:, :, :], ang[:, :, :], 1.0 / two_pi, magic, ALU.mult, ALU.add))
            steps.link(v.tensor_scalar(turns[:, :, :], turns[:, :, :], magic, None, ALU.subtract))
            for c in (c1, c2, c3):
                steps.link(v.scalar_tensor_tensor(out=ang[:, :, :], in0=turns[:, :, :], scalar=-c, in1=ang[:, :, :],
                                                  op0=ALU.mult, op1=ALU.add))
            v.tensor_scalar(ang[:, :, :], ang[:, :, :], pi_in, -pi_in, ALU.min, ALU.max).then_inc(angles, 1)

            steps.link(v.memset(gain_all[:, DEPTH, :], 0.0))
            dve.wait_ge(gains_turned, 1)
            for c, n in GAINS:
                ins = v.tensor_copy(gain_all[:, 0:DEPTH, c:c + n],
                                    sc[0][:, DEPTH * c:DEPTH * (c + n)].rearrange("p (l k) -> p l k", l=DEPTH))
            steps.link(ins)
            v.tensor_copy(gain[:, :], gain_all[:, 0, :]).then_inc(gains_now, 1)

            def lo(pos, upto):
                while state[0] <= upto:
                    p = state[0]
                    dve.wait_ge(hi_ready, pos.count(NP, p + 1, 8))
                    v.tensor_tensor(split_view(w_lo, p), raw_view(p), split_view(w_hi, p).bitcast(F32), ALU.subtract)\
                        .then_inc(lo_ready, 1)
                    state[0] += 1

            def turned_lo(pos, name):
                dve.wait_ge(tp_hi, pos.count(NHI, HI_FILL[name] + 1, 2))
                b, kind = bank(name), name[0]
                if kind == "ckv":
                    for t in range(TT):
                        for k in range(KV):
                            i = 2 * t + k
                            ins = v.scalar_tensor_tensor(
                                out=s2_lo[:, KQ + k, t * P:(t + 1) * P], in0=b[:, i * P:(i + 1) * P],
                                scalar=gain[:, G_KVN + k:G_KVN + k + 1],
                                in1=s2_hi[:, KQ + k, t * P:(t + 1) * P].bitcast(F32), op0=ALU.mult, op1=ALU.subtract)
                    ins.then_inc(tp_done, 1)
                    return
                h, low, k0, nk, t = stationary(name)
                dst = low[:, k0:k0 + nk, t * P:(t + 1) * P]
                hiv = h[:, k0:k0 + nk, t * P:(t + 1) * P].bitcast(F32)
                src = b[:, 0:nk * P].rearrange("p (k n) -> p k n", k=nk)
                col = {"x": G_PRE + k0, "xm": G_MLP + k0, "cq": G_QN}.get(kind)
                if kind == "mix":
                    v.scalar_tensor_tensor(out=dst, in0=src, scalar=0.5, in1=hiv, op0=ALU.mult,
                                           op1=ALU.subtract).then_inc(tp_done, 1)
                elif col is None:
                    v.tensor_tensor(dst, src, hiv, ALU.subtract).then_inc(tp_done, 1)
                else:
                    for k in range(nk):
                        ins = v.scalar_tensor_tensor(out=dst[:, k, :], in0=src[:, k, :],
                                                     scalar=gain[:, col + k:col + k + 1], in1=hiv[:, k, :],
                                                     op0=ALU.mult, op1=ALU.subtract)
                    ins.then_inc(tp_done, 1)

            def turned_copy(pos, name):
                dve.wait_ge(tp_full, pos.count(NF, FILL[name] + 1))
                b = bank(name)
                if name[0] == "kA":
                    ins = v.tensor_copy(kT_a[:, :], b[:, 0:SEQ])
                elif name[0] == "qA":
                    _, t, h = name
                    ins = v.tensor_copy(qT_a[:, 4 * h:4 * h + 4, t * P:(t + 1) * P],
                                        b[:, :].rearrange("p (h n) -> p h n", h=4))
                elif name[0] in ("qB", "kB"):
                    _, t, h = name
                    dst = qT_b if name[0] == "qB" else kT_b
                    ins = v.tensor_copy(dst[:, 4 * h:4 * h + 4, t * P:(t + 1) * P],
                                        b[0:BQK, :].rearrange("p (h n) -> p h n", h=4))
                else:
                    i = name[1]
                    if i >= 2:
                        dve.wait_ge(pv_done, pos.count(NQ, i - 1))
                    if quantum_shape(i)[2]:
                        v.tensor_copy(probsT[0:CHUNK, i % 2, 0:2 * P], b[0:CHUNK, 0:2 * P])
                        ins = v.tensor_copy(probsT[:, i % 2, 2 * P:4 * P], b[:, 2 * P:4 * P])
                    else:
                        ins = v.tensor_copy(probsT[:, i % 2, :], b[:, :])
                ins.then_inc(tp_done, 1)

            def turned(pos, name):
                turned_lo(pos, name) if name[0] in HI_KINDS else turned_copy(pos, name)

            def used(pos, p):
                dve.wait_ge(piece_used, pos.count(NP, RING + p + 1))

            def rs(name):
                c = SUMS[name]
                return rstd[:, c:c + 1]

            def wait_rstd(pos, name):
                dve.wait_ge(rstd_ready, pos.count(NSUM, SUMS[name] + 1))

            def row_maxima(pos, i):
                kind, t, g, h, n = QUANTA[i]
                n, w, skip = quantum_shape(i)
                c = q_col(i)
                dve.wait_ge(scores_ready, pos.count(NQ, i + 1))
                steps.link(v.tensor_reduce(row_max[:, c:c + n],
                                           sc[i % 2][:, :].rearrange("p (h k) -> p h k", h=n)[:, :, skip:w], AX, ALU.max))
                if kind == "A":
                    v.scalar_tensor_tensor(out=neg_m[:, c:c + n], in0=row_max[:, c:c + n], scalar=-SCALE_A,
                                           in1=neg_sink[:, g * AG + h:g * AG + h + n], op0=ALU.mult,
                                           op1=ALU.min).then_inc(neg_max, 1)
                else:
                    v.tensor_scalar(neg_m[:, c:c + n], row_max[:, c:c + n], -SCALE_B, None, ALU.mult).then_inc(neg_max, 1)
                if i in YLAST[:4]:
                    yi = YLAST.index(i)
                    g = yi % 2
                    dve.wait_ge(neg_max, pos.count(NQ, i + 1))
                    v.tensor_tensor(sink_e[:, y_cols(yi)], neg_m[:, y_cols(yi)], neg_sink[:, g * AG:(g + 1) * AG],
                                    ALU.subtract).then_inc(sink_arg, 1)

            def normalise(pos, yi):
                c = y_cols(yi)
                dve.wait_ge(probs_ready, pos.count(NQ, YLAST[yi] + 1))
                if yi < 4:
                    dve.wait_ge(sink_exp, pos.count(4, yi + 1))
                    steps.link(v.tensor_tensor(denom[:, c], row_sum[:, c], sink_e[:, c], ALU.add))
                    steps.link(v.reciprocal(denom[:, c], denom[:, c]))
                    t, g = yi // 2, yi % 2
                    dst = tok[:, t, g * COL:(g + 1) * COL]
                else:
                    steps.link(v.reciprocal(denom[:, c], row_sum[:, c]))
                    dst = latent[:, yi - 4, 0:COL]
                dve.wait_ge(pv_done, pos.count(NQ, YLAST[yi] + 1))
                v.tensor_tensor(dst.rearrange("p (h d) -> p h d", h=8),
                                acc[2 + yi % 2][:, :].rearrange("p (h d) -> p h d", h=8),
                                denom[:, c].unsqueeze(2).to_broadcast([P, 8, 64]), ALU.mult).then_inc(y_out, 1)

            def gate_logits(pos, c):
                used(pos, P_STEP + 4 * c + 3)
                if c == 0:
                    dve.wait_ge(pool_roped, pos.count(8, 8))
                    dve.wait_ge(bias_loaded, pos.count(16, 16))
                gt = gate_a if c < 2 else gate_b
                for t in range(TT):
                    v.scalar_tensor_tensor(out=gt[:, t, (c % 2) * COL:(c % 2 + 1) * COL], in0=acc[t][:, :],
                                           scalar=rs(("x", t)), in1=bias_g[:, c * COL:(c + 1) * COL],
                                           op0=ALU.mult, op1=ALU.add).then_inc(gated_out, 1)

            def gated(pos, p, gt, c, banks):
                used(pos, p)
                for t in range(TT):
                    view = gt[:, t, c * COL:(c + 1) * COL]
                    v.scalar_tensor_tensor(out=view, in0=view, scalar=1.0, in1=banks[t][:, :], op0=ALU.add,
                                           op1=ALU.mult).then_inc(gated_out, 1)

            def update_x(pos, name, which):
                t = name[1]
                wait_rstd(pos, name)
                for c in range(2):
                    cols = slice(c * COL, (c + 1) * COL)
                    steps.link(v.scalar_tensor_tensor(out=probs[:, c, :], in0=acc[2 * c + t][:, :], scalar=rs(name),
                                                      in1=post_g[:, which, cols], op0=ALU.mult, op1=ALU.mult))
                    v.tensor_tensor(x[:, t, cols], x[:, t, cols], probs[:, c, :], ALU.add).then_inc(x_ready[t], 1)
                dve.wait_ge(x_ready[t], pos.count(4, 4 + 2 * which))

            state = [0]
            with dve.Fori(0, DEPTH) as l:
                pos = Pos(l)
                state[0] = 0
                steps.pos, first = pos, steps.n
                steps.per_layer = 40
                dve.wait_ge(gains_now, pos.count(1, 1))
                lo(pos, 1)
                turned(pos, ("x", 0, 0))
                turned(pos, ("x", 0, 1))
                lo(pos, 3)
                turned(pos, ("x", 1, 0))
                turned(pos, ("x", 1, 1))
                for n0, (c0, N, pair, p) in enumerate(((0, BQL, 0, 3), (BQL, BKL + BR, 1, 7))):
                    lo(pos, p + 3)
                    if n0 == 0:
                        for t in range(TT):
                            wait_rstd(pos, ("x", t))
                    used(pos, p)
                    for t in range(TT):
                        v.tensor_scalar(latent[:, t, c0:c0 + N], acc[2 * pair + t][:, 0:N], rs(("x", t)), None,
                                        ALU.mult).then_inc(latent_out, 1)
                lo(pos, 14)
                turned(pos, ("cq", 0))
                turned(pos, ("cq", 1))
                lo(pos, 18)
                turned(pos, ("ckv",))
                dve.wait_ge(tables_ready, 1)
                for c, p in ((0, 18), (1, 22)):
                    lo(pos, p)
                    dve.wait_ge(proj_out, pos.count(14, 2 * PROJ[f"q{c}"] + 1))
                    rope(v, steps, probs[:, 0, :], q_of_group(0, c).rearrange("p h (c d) -> p h c d", c=2), AG, AD // 2, 0, 1)\
                        .then_inc(roped, 1)
                    dve.wait_ge(roped, pos.count(2, c + 1))
                lo(pos, 26)
                dve.wait_ge(sinks_loaded, pos.count(16, 16))
                v.tensor_scalar(neg_sink[:, :], sink_in[:, :], -1.0, None, ALU.mult)
                turned(pos, ("kA",))
                turned(pos, ("qA", 0, 0))
                turned(pos, ("qA", 0, 1))
                lo(pos, 30)
                for i in range(NSTEP):
                    if i % 4 == 0 and 0 < i <= 16:
                        gate_logits(pos, i // 4 - 1)
                    for name in EXTRA.get(i - 1, []):
                        turned(pos, name)
                    if i - 3 in YLAST:
                        normalise(pos, YLAST.index(i - 3))
                    if i < NQ:
                        row_maxima(pos, i)
                    if i >= 2:
                        turned(pos, ("P", i - 2))
                    lo(pos, P_STEP + 3 + i)
                p = P_STEP + NSTEP
                dve.wait_ge(tanh_done, pos.count(4 * TT, 4 * TT))
                gated(pos, p - 1, gate_a, 0, acc[0:2])
                normalise(pos, 5)
                lo(pos, p + 4)
                turned(pos, ("y", 5))
                lo(pos, 53 + 1)
                gated(pos, 51, gate_b, 0, acc[0:2])
                lo(pos, 55 + 1)
                turned(pos, ("mix", 0, 0))
                turned(pos, ("mix", 0, 1))
                gated(pos, 53, gate_a, 1, sc)
                gated(pos, 55, gate_b, 1, acc[2:4])
                lo(pos, 57 + 3)
                turned(pos, ("mix", 1, 0))
                turned(pos, ("mix", 1, 1))
                lo(pos, 63)
                dve.wait_ge(post_loaded, pos.count(32, 32))
                update_x(pos, ("mixpost", 0), 0)
                lo(pos, 65)
                turned(pos, ("xm", 0, 0))
                turned(pos, ("xm", 0, 1))
                update_x(pos, ("mixpost", 1), 0)
                lo(pos, 67)
                turned(pos, ("xm", 1, 0))
                turned(pos, ("xm", 1, 1))
                dve.wait_ge(tp_done, pos.count(NF, 2 + FILL[("xm", 1, 1)] + 1))
                v.tensor_copy(gain[:, :], gain_all[:, l + 1, :]).then_inc(gains_now, 1)
                lo(pos, 72)
                for t in range(TT):
                    turned(pos, ("h", 0, t))
                lo(pos, 79)
                base = 2 * L_LOOP
                with dve.Fori(0, LOOP_J) as j:
                    here = Pos(l, j)
                    lo(here, base + 4)
                    for t in range(TT):
                        turned(here, ("h", 1, t))
                    lo(here, base + 11)
                base += 8 * LOOP_J
                state[0] = base + 4
                lo(pos, base + 4)
                for t in range(TT):
                    turned(pos, ("h", MJ - 2, t))
                lo(pos, base + 8)
                for t in range(TT):
                    turned(pos, ("h", MJ - 1, t))
                lo(pos, NP - 1)
                update_x(pos, ("mlppost", 0), 1)
                update_x(pos, ("mlppost", 1), 1)
                assert steps.n - first == steps.per_layer, steps.n - first

        @block.tensor
        def _(pe):
            mm = nc.tensor.matmul
            pe.sem_inc(piece_used, RING)
            pe.wait_ge(ident_ready, 1)
            pe.wait_ge(gains_loaded, 16 * len(GAINS))
            n = DEPTH * NGAIN
            nc.tensor.transpose(sc[0][:, 0:n], gain_rows[:, :], ident[0:n, 0:n]).then_inc(gains_turned, 1)

            def turn(pos, name, blocks, per_j=0):
                b = bank(name)
                pe.wait_ge(tp_done, pos.count(NF, FILL[name] + 1, 2))
                for i, src in reversed(list(enumerate(blocks))):
                    rows = src.free_size()
                    ins = nc.tensor.transpose(b[0:rows, i * P:(i + 1) * P], src, ident[:, :])
                ins.then_inc(tp_full, 1)

            def turned(pos, name, per_j=0):
                pe.wait_ge(tp_done, pos.count(NF, 2 + FILL[name] + 1, 2))

            def product(pos, p, k0, stat, banks, start=False, stop=False, tiles=(0, 1), release=True, mark=None):
                a, b = piece_rows(p)
                N = LOADS[p // 2][2]
                h, low = stat
                pe.wait_ge(lo_ready, pos.count(NP, 2 * RAW + p + 1, 8))
                wh = split_view(w_hi, p).rearrange("p (k n) -> p k n", k=b - a)
                wl = split_view(w_lo, p).rearrange("p (k n) -> p k n", k=b - a)
                for t in tiles:
                    tk = slice(t * P, (t + 1) * P)
                    for k in range(b - a):
                        kk = k0 + a + k
                        mm(banks[t][:, 0:N], h[:, kk, tk], wh[:, k, :], start=(start and k == 0), stop=False)
                        mm(banks[t][:, 0:N], h[:, kk, tk], wl[:, k, :], start=False, stop=False)
                        ins = mm(banks[t][:, 0:N], low[:, kk, tk], wh[:, k, :], start=False,
                                 stop=(stop and k == b - a - 1))
                if release:
                    ins.then_inc(piece_used, 1)
                elif mark is not None:
                    ins.then_inc(mark, 1)

            s1, s2 = (s1_hi, s1_lo), (s2_hi, s2_lo)

            def turn_x(pos, kind, t):
                pe.wait_ge(x_loaded[t], 16)
                for h in range(2):
                    pe.wait_ge(x_ready[t], pos.count(4, (2 if kind == "xm" else 0) + h + 1))
                    turn(pos, (kind, t, h), [x[:, t, (4 * h + k) * P:(4 * h + k + 1) * P] for k in range(4)])

            def first_product(pos, p0, kind):
                N = LOADS[p0 // 2][2]

                def part(t, xs, ws, pieces, first=False, last=False, release=False):
                    for i in pieces:
                        w = split_view(ws, p0 + i).rearrange("p (k n) -> p k n", k=2)
                        if ws is w_lo:
                            pe.wait_ge(lo_ready, pos.count(NP, 2 * RAW + p0 + i + 1))
                        elif xs is s1_hi:
                            if i % 2 == 0:
                                pe.wait_ge(tp_hi, pos.count(NHI, HI_FILL[(kind, t, i // 2)] + 1))
                            pe.wait_ge(hi_ready, pos.count(NP, p0 + i + 1))
                        for k in range(2):
                            ins = mm(acc[t][:, 0:N], xs[:, 2 * i + k, t * P:(t + 1) * P], w[:, k, :],
                                     start=(first and i == 0 and k == 0), stop=(last and i == 3 and k == 1))
                        if release:
                            ins.then_inc(piece_used, 1)

                turn_x(pos, kind, 0)
                part(0, s1_hi, w_hi, range(4), first=True)
                part(0, s1_hi, w_lo, range(2))
                turned(pos, (kind, 0, 1))
                part(0, s1_lo, w_hi, range(4))
                turn_x(pos, kind, 1)
                part(0, s1_hi, w_lo, range(2, 4), last=True)
                part(1, s1_hi, w_hi, range(4), first=True)
                part(1, s1_hi, w_lo, range(4))
                turned(pos, (kind, 1, 1))
                part(1, s1_lo, w_hi, range(4), last=True, release=True)

            def turn_h(pos, j, at):
                for t in range(TT):
                    pe.wait_ge(h_ready, pos.count(TT * MJ, TT * j + t + 1, TT))
                    turn(pos, ("h", at, t), [tok[:, t, k * P:(k + 1) * P] for k in range(4)])

            def scores(pos, i):
                kind, t, g, h, n = QUANTA[i]
                n, w, skip = quantum_shape(i)
                if i >= 2:
                    pe.wait_ge(probs_ready, pos.count(NQ, i - 1))
                r0, r1 = (64 * g, 64 * g + 64) if kind == "A" else (0, P)
                which = 0 if t == 0 else (1 if kind == "A" else 2)
                b = sc[i % 2]
                view = b[:, :].rearrange("p (h k) -> p h k", h=n)[:, :, skip:w]
                mk = mask[r0:r1, which, skip:w].unsqueeze(1).to_broadcast([r1 - r0, n, w - skip])
                mm(view, chunk_of[r0:r1, :], mk, start=True, stop=False)
                for a in range(n):
                    if kind == "A":
                        q = qT_a[r0:r1, h + a, t * P:(t + 1) * P]
                        k = kT_a[r0:r1, skip:w]
                    else:
                        q = qT_b[:, h + a, t * P:(t + 1) * P]
                        k = kT_b[:, h + a, 0:w]
                    ins = mm(b[:, a * w + skip:(a + 1) * w], q, k, start=False, stop=(a == n - 1))
                ins.then_inc(scores_ready, 1)

            def turn_probs(pos, i):
                n, w, skip = quantum_shape(i)
                pe.wait_ge(probs_ready, pos.count(NQ, i + 1))
                blocks = []
                for b in range(w // P):
                    for a in range(n):
                        blocks.append(probs[:, i % 2, a * w + b * P + (skip if b == 0 else 0):a * w + (b + 1) * P])
                turn(pos, ("P", i), blocks)

            def values(pos, i):
                kind, t, g, h, n = QUANTA[i]
                n, w, skip = quantum_shape(i)
                yi = first_of_y(i)
                turned(pos, ("P", i))
                if i == 0 or i - 1 in YLAST:
                    if yi >= 2:
                        pe.wait_ge(y_out, pos.count(NY, yi - 1))
                y = acc[2 + yi % 2]
                for a in range(n):
                    for b in range(w // P):
                        rows = CHUNK if (skip and b == 0) else P
                        pt = probsT[0:rows, i % 2, (b * n + a) * P:(b * n + a + 1) * P]
                        if kind == "A":
                            vv = v_tail[:, g * AD:(g + 1) * AD] if rows == CHUNK else \
                                kv_a[:, b, (AKV + g) * AD:(AKV + g + 1) * AD]
                        else:
                            vv = v_b[:, b, (h + a) * BV:(h + a + 1) * BV]
                        ins = mm(y[:, (h + a) * 64:(h + a + 1) * 64], pt, vv, start=(b == 0), stop=(b == w // P - 1))
                ins.then_inc(pv_done, 1)

            def extra(pos, name):
                if name[0] == "qA":
                    _, t, h = name
                    blocks = [tok[:, t, (4 * h + a) * AKV * AD:(4 * h + a + 1) * AKV * AD] for a in range(4)]
                elif name[0] in ("qB", "kB"):
                    _, t, h = name
                    src = gate_b if name[0] == "qB" else k_b
                    blocks = [src[:, t, (4 * h + a) * BQK:(4 * h + a + 1) * BQK] for a in range(4)]
                else:
                    yi = name[1]
                    pe.wait_ge(y_out, pos.count(NY, yi + 1))
                    src = tok[:, yi // 2, (yi % 2) * COL:(yi % 2 + 1) * COL] if yi < 4 else latent[:, yi - 4, 0:COL]
                    blocks = [src[:, k * P:(k + 1) * P] for k in range(4)]
                turn(pos, name, blocks)

            def projected(pos, name):
                pe.wait_ge(proj_out, pos.count(14, 2 * PROJ[name] + 2))

            def gate_free(pos, name):
                pe.wait_ge(gated_out, pos.count(16, 2 * GATED[name] + 2))

            pair = [acc[0:2], acc[2:4]]
            with pe.Fori(0, DEPTH) as l:
                pos = Pos(l)
                first_product(pos, 0, "x")
                for i, p in enumerate(range(4, 8)):
                    product(pos, p, 4 * (i // 2), s1, pair[1], i == 0, i == 3)
                pe.wait_ge(latent_out, pos.count(2 * TT, TT))
                for i, p in enumerate(range(8, 12)):
                    product(pos, p, 4 * (i // 2), s1, pair[0], i == 0, i == 3)
                for t in range(TT):
                    turn(pos, ("cq", t), [latent[:, t, k * P:(k + 1) * P] for k in range(KQ)])
                pe.wait_ge(latent_out, pos.count(2 * TT, 2 * TT))
                for i, p in enumerate(range(12, 16)):
                    product(pos, p, 4 * (i // 2), s1, pair[1], i == 0, i == 3)
                turn(pos, ("ckv",), [latent[:, t, BQL + k * P:BQL + (k + 1) * P] for t in range(TT) for k in range(KV)])
                projected(pos, "kv")
                for i, p in enumerate(range(16, 20)):
                    product(pos, p, 4 * (i // 2), s1, pair[0], i == 0, i == 3)
                turned(pos, ("ckv",))
                for c, (q, before, k0) in enumerate((("uq0", "q0", 0), ("uq1", "q1", 0), ("ukv0", "uq0", KQ), ("ukv1", "uq1", KQ))):
                    if c == 3:
                        pe.wait_ge(pool_roped, pos.count(8, 2 * POOL_ROPED["kA"] + 2))
                        turn(pos, ("kA",), [kv_a[:, t, 0:AKV * AD] for t in range(TT)])
                        pe.wait_ge(roped, pos.count(2, 2))
                        extra(pos, ("qA", 0, 0))
                        extra(pos, ("qA", 0, 1))
                    projected(pos, before)
                    for i in range(2):
                        product(pos, 20 + 2 * c + i, k0, s2, pair[1 - c % 2], i == 0, i == 1)
                turned(pos, ("qA", 0, 1))
                pe.wait_ge(consts_ready, 2)
                for i in range(NSTEP):
                    if i < NQ:
                        scores(pos, i)
                    if i >= 2:
                        turn_probs(pos, i - 2)
                    if i == 0:
                        projected(pos, "ukv1")
                    p = P_STEP + i
                    if i % 4 == 0 and i > 0:
                        gate_free(pos, f"g{i // 4 - 1}")
                    if i < 16:
                        product(pos, p, 4 * (i % 4 // 2), s1, pair[0], i % 4 == 0, i % 4 == 3)
                    else:
                        if i == 16:
                            turned(pos, ("y", 3))
                        product(pos, p, 4 * (i % 4 // 2), s2, pair[0], i % 4 == 0, i % 4 == 3)
                    if i >= 2:
                        values(pos, i - 2)
                    for name in EXTRA.get(i, []):
                        if i in (1, 3):
                            pe.wait_ge(pool_roped, pos.count(8, 6 if i == 1 else 8))
                        extra(pos, name)
                product(pos, 48, 0, s2, sc, True, False)
                extra(pos, ("y", 5))
                product(pos, 49, 0, s2, sc)
                gate_free(pos, "oa0")
                turned(pos, ("y", 5))
                product(pos, 50, 4, s1, pair[0], True, False)
                product(pos, 51, 4, s1, pair[0], False, True)
                product(pos, 52, 4, s2, sc)
                product(pos, 53, 4, s2, sc, False, True)
                for t in range(TT):
                    pe.wait_ge(mixed, pos.count(4, t + 1))
                    turn(pos, ("mix", 0, t), [tok[:, t, k * P:(k + 1) * P] for k in range(4)])
                product(pos, 54, 4, s1, pair[1], True, False)
                product(pos, 55, 4, s1, pair[1], False, True)
                turned(pos, ("mix", 0, 1))
                product(pos, 56, 0, s1, pair[0], True)
                product(pos, 57, 0, s1, pair[0])
                for t in range(TT):
                    pe.wait_ge(mixed, pos.count(4, 2 + t + 1))
                    turn(pos, ("mix", 1, t), [tok[:, t, COL + k * P:COL + (k + 1) * P] for k in range(4)])
                product(pos, 58, 0, s1, pair[1], True)
                product(pos, 59, 0, s1, pair[1])
                turned(pos, ("mix", 1, 1))

                def finish(pos, p, k0, stat):
                    for t in range(TT):
                        for i in range(4):
                            product(pos, p + i, k0, stat, pair[i // 2], False, i % 2 == 1, tiles=(t,), release=(t == 1),
                                    mark=tile0_done if i % 2 == 1 else None)

                finish(pos, 60, 4, s1)

                def mlp_in(pos, p, banks, j, at):
                    for i in range(4):
                        if i == 2:
                            turn_h(pos, j, at)
                        product(pos, p + i, 4 * (i // 2), s1, banks, i == 0, i == 3)

                def mlp_out(pos, p, start=False):
                    for i in range(4):
                        product(pos, p + i, 0, s2, pair[i // 2], start and i % 2 == 0)

                first_product(pos, 2 * L_MLP, "xm")
                mlp_in(pos, 68, sc, 0, 0)
                turned(pos, ("h", 0, 1))
                mlp_out(pos, 72, start=True)
                with pe.Fori(0, LOOP_J) as j:
                    here = Pos(l, j)
                    pe.wait_ge(relu_done, here.count(TT * MJ, 2 * TT, TT))
                    mlp_in(here, 76, sc, 1, 1)
                    turned(here, ("h", 1, 1))
                    mlp_out(here, 80)
                base = 2 * L_LOOP + 8 * LOOP_J
                pe.wait_ge(relu_done, pos.count(TT * MJ, TT * (MJ - 1)))
                mlp_in(pos, base, sc, MJ - 2, MJ - 2)
                turned(pos, ("h", MJ - 2, 1))
                product(pos, base + 4, 0, s2, pair[0])
                product(pos, base + 5, 0, s2, pair[0])
                turn_h(pos, MJ - 1, MJ - 1)
                product(pos, base + 6, 0, s2, pair[1])
                product(pos, base + 7, 0, s2, pair[1])
                turned(pos, ("h", MJ - 1, 1))
                finish(pos, base + 8, 4, s2)


_INS = ["x", "positions", "g_mix_pre", "g_mix_post", "g_mlp_pre", "g_mlp_post", "w_in", "b_gate", "sinks",
        "q_norm", "kv_norm", "w_uq", "w_ukv", "w_oa", "w_ob", "w_out", "w_mlp_in", "w_mlp_out"]


def kernel(**inputs):
    import concourse.bacc as bacc
    from concourse.bass_utils import run_bass_kernel_spmd

    nc = bacc.Bacc("TRN2", target_bir_lowering=False, num_devices=1)
    arrays, args = {}, []
    for name in _INS:
        a = np.ascontiguousarray(inputs[name])
        arrays["in_" + name] = a
        args.append(nc.dram_tensor("in_" + name, a.shape, mybir.dt.from_np(a.dtype), kind="ExternalInput").ap())
    out = nc.dram_tensor("out_x", (1, SEQ, D), F32, kind="ExternalOutput").ap()
    build(nc, *args, out)
    result = run_bass_kernel_spmd(nc, [arrays], core_ids=[0])
    return result.results[0]["out_x"]
```

```python
from contextlib import ExitStack

import concourse.bass as bass
import numpy as np
from concourse import mybir

F32 = mybir.dt.float32
F32R = mybir.dt.float32r
I32 = mybir.dt.int32
BF16 = mybir.dt.bfloat16
ALU = mybir.AluOpType
ACT = mybir.ActivationFunctionType
AX = mybir.AxisListType.X

P = 128
D = 1024
SEQ = 256
DEPTH = 2
CHUNK = 64
TT = SEQ // P
KD = D // P
EPS = 1e-6
THETA = 10000.0
NEG = -1e30
AH, AKV, AD = 16, 2, 64
AG = AH // AKV
BH, BQL, BKL, BN, BR, BV = 8, 384, 256, 64, 32, 64
BQK = BN + BR
DFF = 4 * D
COL = 512
KQ, KV = BQL // P, BKL // P
C_Q, C_KV, C_CQ = 0, AH * AD, AH * AD + 2 * AKV * AD
C_CKV = C_CQ + BQL
C_GATE = C_CKV + BKL + BR
SCALE_A = AD ** -0.5
SCALE_B = BQK ** -0.5
NGAIN = KD + KD + KQ + KV
G_PRE, G_MLP, G_QN, G_KVN = 0, KD, 2 * KD, 2 * KD + KQ
GAINS = ((G_PRE, KD), (G_MLP, KD), (G_QN, KQ), (G_KVN, KV))

LOADS = (
    [("cq", 4, BQL)] * 2 + [("ckv", 4, BKL + BR)] * 2 + [("kv", 4, 2 * AKV * AD)] * 2
    + [("q", 4, COL)] * 4 + [("uq", KQ, BQL)] * 2 + [("ukv", KV, COL)] * 2
    + [("gate", 4, COL)] * 8 + [("oa", 4, COL)] * 3 + [("ob", 4, COL)] + [("oa", 4, COL)] + [("ob", 4, COL)]
    + [("out", 4, COL)] * 4 + [("mlp", 4, COL)] * 32)
NL = len(LOADS)
NP = 2 * NL
RAW = 4
RING = 4
MJ = DFF // COL
L_MLP = 32
L_LOOP = L_MLP + 6
LOOP_J = MJ - 3
assert NL == 64 and LOADS[L_MLP][0] == "mlp" and LOADS[L_MLP - 1][0] == "out"


def piece_rows(p):
    nk = LOADS[p // 2][1]
    cut = (nk + 1) // 2
    return (0, cut) if p % 2 == 0 else (cut, nk)


QUANTA = ([("A", 0, g, h, 4) for g in range(AKV) for h in (0, 4)]
          + [("A", 1, g, h, 2) for g in range(AKV) for h in (0, 2, 4, 6)]
          + [("B", 0, 0, h, 4) for h in (0, 4)] + [("B", 1, 0, h, 2) for h in (0, 2, 4, 6)])
NQ = len(QUANTA)
NSTEP = NQ + 2
P_STEP = 28
YLAST = [1, 3, 7, 11, 13, 17]
NY = len(YLAST)
EXTRA = {1: [("qA", 1, 0)], 2: [("qA", 1, 1)],
         3: [("kB", 0, 0)], 4: [("qB", 0, 0)], 5: [("kB", 0, 1)], 6: [("qB", 0, 1), ("y", 0)],
         7: [("kB", 1, 0)], 8: [("qB", 1, 0), ("y", 1)], 9: [("kB", 1, 1)], 10: [("qB", 1, 1)],
         12: [("y", 2)], 15: [("y", 3)], 18: [("y", 4)]}


def fill_order():
    out = [("x", t, h) for t in range(TT) for h in range(2)]
    out += [("cq", 0), ("cq", 1), ("ckv",), ("kA",), ("qA", 0, 0), ("qA", 0, 1)]
    for i in range(NSTEP):
        if i >= 2:
            out.append(("P", i - 2))
        out += EXTRA.get(i, [])
    out += [("y", 5)] + [("mix", c, t) for c in range(2) for t in range(TT)]
    out += [("xm", t, h) for t in range(TT) for h in range(2)]
    out += [("h", t) for t in range(TT)]
    return out


FILLS = fill_order()
NF = len(FILLS)
FILL = {name: i for i, name in enumerate(FILLS)}
HI_KINDS = ("x", "cq", "ckv", "y", "mix", "xm", "h")
HI_FILL = {name: i for i, name in enumerate(f for f in FILLS if f[0] in HI_KINDS)}
NHI = len(HI_FILL)
assert NF % 2 == 0

PROJ = {n: i for i, n in enumerate(("kv", "q0", "q1", "uq0", "uq1", "ukv0", "ukv1"))}
POOL_ROPED = {n: i for i, n in enumerate(("kA", "kpe", "q", "qB"))}
GATED = {n: i for i, n in enumerate(("g0", "g1", "g2", "g3", "oa0", "ob0", "oa1", "ob1"))}
SUMS = {n: i for i, n in enumerate((s, t) for s in ("x", "cq", "ckv", "mixpost", "xm", "mlppost") for t in range(TT))}
NSUM = len(SUMS)
SUM_PARTS = [(n, h) for n in SUMS for h in range(2 if n[0] in ("mixpost", "mlppost") else 1)]
NPART = len(SUM_PARTS)
WIDTH = {"x": D, "cq": BQL, "ckv": BKL, "mixpost": D, "xm": D, "mlppost": D}


class Pos:

    def __init__(self, l, j=None):
        self.l, self.j = l, j

    def count(self, per_layer, n, per_j=0):
        value = self.l * per_layer + n
        return value if self.j is None else value + self.j * per_j


class Steps:

    def __init__(self, eng, sem, per_layer=0, per_j=0):
        self.eng, self.sem, self.per_layer, self.per_j, self.n, self.pos = eng, sem, per_layer, per_j, 0, None

    def link(self, instruction):
        instruction.then_inc(self.sem, 1)
        self.n += 1
        self.eng.wait_ge(self.sem, self.n if self.pos is None else self.pos.count(self.per_layer, self.n, self.per_j))


def build(nc, x_d, pos_d, g_mix_pre, g_mix_post, g_mlp_pre, g_mlp_post, w_in, b_gate, sinks_d, q_norm,
          kv_norm, w_uq, w_ukv, w_oa, w_ob, w_out, w_mlp_in, w_mlp_out, out_d):
    ctx = ExitStack()
    with ctx:
        def sb(name, shape, dt=F32):
            return ctx.enter_context(nc.sbuf_tensor(name, shape, dt))

        def sem(name):
            return ctx.enter_context(nc.semaphore(name))

        raw = sb("raw", [P, RAW, 4 * COL])
        w_hi = sb("w_hi", [P, RING, 2 * COL], F32R)
        w_lo = sb("w_lo", [P, RING, 2 * COL], F32R)
        s1_hi = sb("s1_hi", [P, KD, SEQ], F32R)
        s1_lo = sb("s1_lo", [P, KD, SEQ], F32R)
        s2_hi = sb("s2_hi", [P, KD, SEQ], F32R)
        s2_lo = sb("s2_lo", [P, KD, SEQ], F32R)
        x = sb("x", [P, TT, D])
        tok = sb("tok", [P, TT, D])
        gate_a = sb("gate_a", [P, TT, D])
        gate_b = sb("gate_b", [P, TT, D])
        k_b = sb("k_b", [P, TT, BH * BQK])
        latent = sb("latent", [P, TT, BQL + BKL + BR])
        kv_a = sb("kv_a", [P, TT, 2 * AKV * AD])
        v_tail = sb("v_tail", [CHUNK, AKV * AD])
        v_b = sb("v_b", [P, TT, BH * BV])
        qT_a = sb("qT_a", [P, AG, SEQ])
        kT_a = sb("kT_a", [P, SEQ])
        qT_b = sb("qT_b", [BQK, BH, SEQ])
        kT_b = sb("kT_b", [BQK, BH, SEQ])
        probs = sb("probs", [P, 2, COL])
        probsT = sb("probsT", [P, 2, COL])
        neg_m = sb("neg_m", [P, TT * (AH + BH)])
        row_max = sb("row_max", [P, TT * (AH + BH)])
        row_sum = sb("row_sum", [P, TT * (AH + BH)])
        sink_e = sb("sink_e", [P, TT * AH])
        denom = sb("denom", [P, TT * (AH + BH)])
        neg_sink = sb("neg_sink", [P, AH])
        sink_in = sb("sink_in", [P, AH])
        bias_g = sb("bias_g", [P, 2 * D])
        post_g = sb("post_g", [P, 2, D])
        squares = sb("squares", [P, 2, D], BF16)
        sums = sb("sums", [P, 2, NSUM])
        var = sb("var", [P, NSUM])
        rstd = sb("rstd", [P, NSUM])
        norm_k = sb("norm_k", [P, 3, 1])
        rstd2 = sb("rstd2", [P, TT])
        rstd2_mean = sb("rstd2_mean", [P, TT])
        gain_rows = sb("gain_rows", [DEPTH * NGAIN, P])
        gain_all = sb("gain_all", [P, DEPTH + 1, NGAIN])
        gain = sb("gain", [P, NGAIN])
        ident = sb("ident", [P, P])
        chunk_of = sb("chunk_of", [P, P], F32R)
        mask = sb("mask", [P, 3, 2 * P], F32R)
        pos_i = sb("pos_i", [P, TT], I32)
        pos_f = sb("pos_f", [P, TT])
        freq = sb("freq", [P, AD // 2])
        ang = sb("ang", [P, TT, AD // 2])
        turns = sb("turns", [P, TT, AD // 2])
        cost = sb("cost", [P, TT, AD // 2])
        sint = sb("sint", [P, TT, 2, AD // 2])

        acc = [ctx.enter_context(nc.psum_tensor(f"acc{i}", [P, COL], F32)) for i in range(4)]
        sc = [ctx.enter_context(nc.psum_tensor(f"sc{i}", [P, COL], F32)) for i in range(2)]
        tp = [ctx.enter_context(nc.psum_tensor(f"tp{i}", [P, COL], F32)) for i in range(2)]

        raw_full = [sem(f"raw_full{i}") for i in range(RAW)]
        hi_ready = sem("hi_ready")
        lo_ready = sem("lo_ready")
        piece_used = sem("piece_used")
        tile0_done = sem("tile0_done")
        tp_full = sem("tp_full")
        tp_hi = sem("tp_hi")
        tp_done = sem("tp_done")
        x_loaded = [sem(f"x_loaded{t}") for t in range(TT)]
        x_ready = [sem(f"x_ready{t}") for t in range(TT)]
        sums_ready = sem("sums_ready")
        rstd_ready = sem("rstd_ready")
        latent_out = sem("latent_out")
        proj_out = sem("proj_out")
        roped = sem("roped")
        pool_roped = sem("pool_roped")
        scores_ready = sem("scores_ready")
        neg_max = sem("neg_max")
        sink_arg = sem("sink_arg")
        sink_exp = sem("sink_exp")
        probs_ready = sem("probs_ready")
        pv_done = sem("pv_done")
        y_out = sem("y_out")
        gated_out = sem("gated_out")
        tanh_done = sem("tanh_done")
        mixed = sem("mixed")
        relu_done = sem("relu_done")
        h_ready = sem("h_ready")
        rstd2_ready = sem("rstd2_ready")
        h_hi = sem("h_hi")
        h_split = sem("h_split")
        gains_loaded = sem("gains_loaded")
        gains_turned = sem("gains_turned")
        gains_now = sem("gains_now")
        sinks_loaded = sem("sinks_loaded")
        bias_loaded = sem("bias_loaded")
        post_loaded = sem("post_loaded")
        pos_loaded = sem("pos_loaded")
        ident_ready = sem("ident_ready")
        consts_ready = sem("consts_ready")
        tables_ready = sem("tables_ready")
        freq_ready = sem("freq_ready")
        angles = sem("angles")
        sines = sem("sines")
        vec_step = sem("vec_step")
        pool_step = sem("pool_step")
        act_step = sem("act_step")
        stored = [sem(f"stored{i}") for i in range(2 * TT)]

        def raw_view(p):
            n, N = p // 2, LOADS[p // 2][2]
            k0, k1 = piece_rows(p)
            return raw[:, n % RAW, k0 * N:k1 * N]

        def split_view(buf, p):
            k0, k1 = piece_rows(p)
            return buf[:, p % RING, 0:(k1 - k0) * LOADS[p // 2][2]]

        def stationary(name):
            kind = name[0]
            if kind in ("x", "xm"):
                _, t, h = name
                return s1_hi, s1_lo, 4 * h, 4, t
            if kind == "cq":
                return s2_hi, s2_lo, 0, KQ, name[1]
            if kind == "y":
                yi = name[1]
                if yi < 4:
                    return s2_hi, s2_lo, 4 * (yi % 2), 4, yi // 2
                return s1_hi, s1_lo, 4, 4, yi - 4
            if kind == "mix":
                return s1_hi, s1_lo, 4 * name[1], 4, name[2]
            if kind == "h":
                return s2_hi, s2_lo, 0, 4, name[1]

        def bank(name):
            return tp[FILL[name] % 2]

        def bank_of_h(buf, b):
            return buf[:, b, 0:COL].rearrange("p (k n) -> p k n", k=2)

        def q_col(i):
            kind, t, g, h, n = QUANTA[i]
            return t * AH + g * AG + h if kind == "A" else TT * AH + t * BH + h

        def q_of_group(t, g):
            return tok[:, t, :].rearrange("p (h g d) -> p g h d", g=AKV, h=AG)[:, g, :, :]

        def y_cols(yi):
            c = 8 * yi
            return slice(c, c + 8)

        def quantum_shape(i):
            kind, t, g, h, n = QUANTA[i]
            return n, COL // n, (CHUNK if kind == "A" and t == 1 else 0)

        def first_of_y(i):
            return next(y for y in range(NY) if i <= YLAST[y])

        def rope(eng, steps, scratch, q, heads, half, t, stride, copies=None):
            n = 2 * heads * half
            tmp = scratch[:, 0:n].rearrange("p (h c d) -> p h c d", h=heads, c=2)
            sn = sint[:, t, :, ::stride].unsqueeze(1).to_broadcast([P, heads, 2, half])
            cs = cost[:, t, ::stride].unsqueeze(1).unsqueeze(1).to_broadcast([P, heads, 2, half])
            steps.link(eng.tensor_tensor(tmp, q[:, :, ::-1, :], sn, ALU.mult))
            steps.link(eng.tensor_tensor(q, q, cs, ALU.mult))
            if copies is None:
                return eng.tensor_tensor(q, q, tmp, ALU.add)
            a, b = (u.rearrange("p h c d -> p h (c d)").to_broadcast(list(copies.shape)) for u in (q, tmp))
            return eng.tensor_tensor(copies, a, b, ALU.add)

        block = ctx.enter_context(nc.Block())

        @block.sync
        def _(sp):
            sp.dma_start(pos_i[:, :], pos_d[0].rearrange("(t p) -> p t", p=P),
                         allow_slow_non_contiguous=True).then_inc(pos_loaded, 16)
            sp.dma_start(x[:, 0, :], x_d[0, 0:P, :]).then_inc(x_loaded[0], 16)
            for src, (c, n) in zip((g_mix_pre, g_mlp_pre, q_norm, kv_norm), GAINS):
                sp.dma_start(gain_rows[DEPTH * c:DEPTH * (c + n), :],
                             src.rearrange("l (k p) -> (l k) p", p=P)).then_inc(gains_loaded, 16)

            def raw_free(pos, n):
                sp.wait_ge(lo_ready, pos.count(NP, 2 * n + 2, 8))

            def load(pos, n, src, wait=True):
                _, nk, N = LOADS[n]
                if wait:
                    raw_free(pos, n)
                sp.dma_start(raw[:, n % RAW, 0:nk * N].rearrange("p (k n) -> p k n", k=nk),
                             src.rearrange("(k p) n -> p k n", p=P)).then_inc(raw_full[n % RAW], 16)

            with sp.Fori(0, DEPTH) as l:
                pos = Pos(l)
                w = w_in[l]
                n = 0
                for c0, N in ((C_CQ, BQL), (C_CKV, BKL + BR), (C_KV, 2 * AKV * AD), (0, COL), (COL, COL)):
                    for h in range(2):
                        if n == 6:
                            raw_free(pos, n)
                            sp.dma_start(sink_in[:, :], sinks_d[l].partition_broadcast(P)).then_inc(sinks_loaded, 16)
                        load(pos, n, w[h * COL:(h + 1) * COL, c0:c0 + N], wait=n != 6)
                        n += 1
                for c in range(2):
                    load(pos, n, w_uq[l][:, c * BQL:(c + 1) * BQL])
                    n += 1
                for c in range(2):
                    load(pos, n, w_ukv[l][:, c * COL:(c + 1) * COL])
                    n += 1
                sp.dma_start(bias_g[:, :], b_gate[l].rearrange("a d -> (a d)").partition_broadcast(P))\
                    .then_inc(bias_loaded, 16)
                for c in range(4):
                    if c == 3:
                        for i, src in enumerate((g_mix_post, g_mlp_post)):
                            sp.dma_start(post_g[:, i, :], src[l].partition_broadcast(P)).then_inc(post_loaded, 16)
                    for h in range(2):
                        load(pos, n, w[h * COL:(h + 1) * COL, C_GATE + c * COL:C_GATE + (c + 1) * COL])
                        n += 1
                for src, h, c in ((w_oa, 0, 0), (w_oa, 1, 0), (w_oa, 0, 1), (w_ob, 0, 0), (w_oa, 1, 1), (w_ob, 0, 1),
                                  (w_out, 0, 0), (w_out, 0, 1), (w_out, 1, 0), (w_out, 1, 1)):
                    load(pos, n, src[l][h * COL:(h + 1) * COL, c * COL:(c + 1) * COL])
                    n += 1
                assert n == L_MLP

                def mlp_in(pos, n, j):
                    for h in range(2):
                        load(pos, n + h, w_mlp_in[l][h * COL:(h + 1) * COL, bass.ts(j, COL)])

                def mlp_out(pos, n, j):
                    for c in range(2):
                        load(pos, n + c, w_mlp_out[l][bass.ts(j, COL), c * COL:(c + 1) * COL])

                mlp_in(pos, n, 0)
                mlp_in(pos, n + 2, 1)
                mlp_out(pos, n + 4, 0)
                with sp.Fori(0, LOOP_J) as j:
                    here = Pos(l, j)
                    mlp_in(here, L_LOOP, j + 2)
                    mlp_out(here, L_LOOP + 2, j + 1)
                n = L_LOOP + 4 * LOOP_J
                mlp_in(pos, n, MJ - 1)
                mlp_out(pos, n + 2, MJ - 2)
                mlp_out(pos, n + 4, MJ - 1)
                assert n + 6 == NL
            for t in range(TT):
                for c in range(2):
                    sp.wait_ge(x_ready[t], 4 * DEPTH + c + 1)
                    cols = slice(c * COL, (c + 1) * COL)
                    sp.dma_start(out_d[0, t * P:(t + 1) * P, cols], x[:, t, cols]).then_inc(stored[2 * t + c], 16)
            for done in stored:
                sp.wait_ge(done, 16)

        @block.gpsimd
        def _(pool):
            g = nc.gpsimd
            steps = Steps(pool, pool_step)

            inv = np.float32(THETA) ** (-np.arange(0, AD, 2, dtype=np.float32) / np.float32(AD))
            for i in range(AD // 2):
                ins = g.memset(freq[:, i:i + 1], float(inv[i]))
            ins.then_inc(freq_ready, 1)
            pool.wait_ge(freq_ready, 1)
            steps.link(g.memset(ident[:, :], 0.0))
            g.affine_select(out=ident[:, :], in_=ident[:, :], compare_op=ALU.not_equal, fill=1.0,
                            base=0, pattern=[[-1, P]], channel_multiplier=1).then_inc(ident_ready, 1)
            pool.wait_ge(ident_ready, 1)
            for i, value in enumerate([EPS, -0.5, D ** -0.5]):
                ins = g.memset(norm_k[:, i], value)
            steps.link(ins)

            sel, mk = chunk_of[:, :].bitcast(F32), mask[:, :, :].bitcast(F32)
            steps.link(g.memset(sel, 0.0))
            steps.link(g.memset(mk, 0.0))
            for half in range(2):
                r = 2 * 32 * half
                steps.link(g.memset(sel[r:r + 1, 0:CHUNK], 1.0))
                steps.link(g.memset(sel[r + 32:r + 33, CHUNK:P], 1.0))
                steps.link(g.memset(mk[r:r + 1, 0, CHUNK:P], NEG))
                steps.link(g.memset(mk[r:r + 1, 1:3, P + CHUNK:2 * P], NEG))
                g.memset(mk[r + 32:r + 33, 1, CHUNK:P], NEG).then_inc(consts_ready, 1)
                pool.wait_ge(consts_ready, half + 1)

            pool.wait_ge(sines, 2)
            steps.link(g.tensor_tensor(cost[:, :, :], turns[:, :, :], turns[:, :, :], ALU.mult))
            steps.link(g.tensor_scalar(cost[:, :, :], cost[:, :, :], -2.0, 1.0, ALU.mult, ALU.add))
            g.tensor_scalar(sint[:, :, 0, :], sint[:, :, 1, :], -1.0, None, ALU.mult).then_inc(tables_ready, 1)
            pool.wait_ge(tables_ready, 1)

            def to_rstd(pos, name):
                c = SUMS[name]
                v = var[:, c:c + 1]
                pool.wait_ge(sums_ready, pos.count(NPART, SUM_PARTS.index((name, 0)) + 1))
                steps.link(g.tensor_tensor(v, sums[:, 0, c:c + 1], norm_k[:, 0], ALU.add))
                if (name, 1) in SUM_PARTS:
                    pool.wait_ge(sums_ready, pos.count(NPART, SUM_PARTS.index((name, 1)) + 1))
                    steps.link(g.tensor_tensor(v, v, sums[:, 1, c:c + 1], ALU.add))
                g.tensor_tensor(rstd[:, c:c + 1], v, norm_k[:, 1], ALU.pow).then_inc(rstd_ready, 1)

            def pool_rope(q, heads, half, t, stride, copies=None):
                return rope(g, steps, gate_a[:, 1, 0:COL], q, heads, half, t, stride, copies)

            def square(pos, j):
                for t in range(TT):
                    pool.wait_ge(relu_done, pos.count(TT * MJ, TT * j + t + 1, TT))
                    if j > 1:
                        pool.wait_ge(h_split, pos.count(TT * (MJ - 1), TT * (j - 2) + t + 1, TT))
                    g.tensor_tensor(tok[:, t, 0:COL], k_b[:, t, 0:COL], k_b[:, t, 0:COL], ALU.mult).then_inc(h_ready, 1)

            origin = steps.n
            with pool.Fori(0, DEPTH) as l:
                pos = Pos(l)
                steps.per_layer = 33
                steps.pos, first = pos, steps.n
                for t in range(TT):
                    to_rstd(pos, ("x", t))
                for t in range(TT):
                    to_rstd(pos, ("cq", t))
                for t in range(TT):
                    to_rstd(pos, ("ckv", t))
                for t in range(TT):
                    pool.wait_ge(proj_out, pos.count(14, 2 * PROJ["kv"] + t + 1))
                    pool_rope(kv_a[:, t, 0:AKV * AD].rearrange("p (h c d) -> p h c d", h=AKV, c=2), AKV, AD // 2, t, 1)\
                        .then_inc(pool_roped, 1)
                    pool.wait_ge(pool_roped, pos.count(8, t + 1))
                for t in range(TT):
                    pool.wait_ge(latent_out, pos.count(2 * TT, TT + t + 1))
                    kp = latent[:, t, BQL + BKL:BQL + BKL + BR]
                    pool_rope(kp.rearrange("p (h c d) -> p h c d", h=1, c=2), 1, BR // 2, t, 2,
                              copies=k_b[:, t, :].rearrange("p (h d) -> p h d", h=BH)[:, :, BN:BQK])\
                        .then_inc(pool_roped, 1)
                    pool.wait_ge(pool_roped, pos.count(8, 2 * POOL_ROPED["kpe"] + t + 1))
                for c in range(2):
                    pool.wait_ge(proj_out, pos.count(14, 2 * PROJ[f"q{c}"] + 2))
                    pool_rope(q_of_group(1, c).rearrange("p h (c d) -> p h c d", c=2), AG, AD // 2, 1, 1)\
                        .then_inc(pool_roped, 1)
                    pool.wait_ge(pool_roped, pos.count(8, 2 * POOL_ROPED["q"] + c + 1))
                for t in range(TT):
                    pool.wait_ge(proj_out, pos.count(14, 2 * PROJ["uq1"] + t + 1))
                    qb = gate_b[:, t, 0:BH * BQK].rearrange("p (h d) -> p h d", h=BH)[:, :, BN:BQK]
                    pool_rope(qb.rearrange("p h (c d) -> p h c d", c=2), BH, BR // 2, t, 2).then_inc(pool_roped, 1)
                    pool.wait_ge(pool_roped, pos.count(8, 2 * POOL_ROPED["qB"] + t + 1))
                for c in range(2):
                    cols = slice(c * COL, (c + 1) * COL)
                    for t in range(TT):
                        pool.wait_ge(gated_out, pos.count(16, 2 * GATED[f"ob{c}"] + t + 1))
                        g.tensor_tensor(tok[:, t, cols], gate_a[:, t, cols], gate_b[:, t, cols], ALU.add)\
                            .then_inc(mixed, 1)
                for name in ("mixpost", "xm"):
                    for t in range(TT):
                        to_rstd(pos, (name, t))
                c = SUMS[("xm", 0)]
                pool.wait_ge(rstd_ready, pos.count(NSUM, c + 2))
                steps.link(g.tensor_tensor(rstd2[:, :], rstd[:, c:c + TT], rstd[:, c:c + TT], ALU.mult))
                g.tensor_tensor(rstd2_mean[:, :], rstd2[:, :], norm_k[:, 2].to_broadcast([P, TT]), ALU.mult)\
                    .then_inc(rstd2_ready, 1)
                square(pos, 0)
                square(pos, 1)
                with pool.Fori(0, LOOP_J) as j:
                    square(Pos(l, j), 2)
                square(pos, MJ - 1)
                for t in range(TT):
                    to_rstd(pos, ("mlppost", t))
                assert steps.n - first == steps.per_layer, steps.n - first

        @block.scalar
        def _(act):
            s = nc.scalar
            steps = Steps(act, act_step)
            act.wait_ge(angles, 1)
            s.activation(sint[:, :, 1, :], ang[:, :, :], ACT.Sin).then_inc(sines, 1)
            s.activation(turns[:, :, :], ang[:, :, :], ACT.Sin, scale=0.5).then_inc(sines, 1)

            act.wait_ge(x_loaded[0], 16)
            act.dma_start(x[:, 1, :], x_d[0, P:2 * P, :]).then_inc(x_loaded[1], 16)

            act.wait_ge(sines, 2)
            s.activation(neg_m[:, 0:1], turns[:, 0, 0:1], ACT.Exp)

            def hi(pos, upto):
                while state[0] <= upto:
                    p = state[0]
                    n = p // 2
                    if p % 2 == 0:
                        act.wait_ge(raw_full[n % RAW], pos.count(16 * NL // RAW, 16 * (n // RAW + 1), 16))
                    act.wait_ge(piece_used, pos.count(NP, p + 1, 8))
                    s.copy(split_view(w_hi, p), raw_view(p)).then_inc(hi_ready, 1)
                    state[0] += 1

            def turned_hi(pos, name):
                act.wait_ge(tp_full, pos.count(NF, FILL[name] + 1))
                b, kind = bank(name), name[0]
                if kind == "ckv":
                    for t in range(TT):
                        for k in range(KV):
                            i = 2 * t + k
                            ins = s.activation(s2_hi[:, KQ + k, t * P:(t + 1) * P], b[:, i * P:(i + 1) * P], ACT.Copy,
                                               scale=gain[:, G_KVN + k:G_KVN + k + 1])
                    ins.then_inc(tp_hi, 1)
                    return
                h, _, k0, nk, t = stationary(name)
                dst = h[:, k0:k0 + nk, t * P:(t + 1) * P]
                src = b[:, 0:nk * P].rearrange("p (k n) -> p k n", k=nk)
                col = {"x": G_PRE + k0, "xm": G_MLP + k0, "cq": G_QN}.get(kind)
                if col is None:
                    s.activation(dst, src, ACT.Copy, scale=0.5 if kind == "mix" else 1.0).then_inc(tp_hi, 1)
                    return
                for k in range(nk):
                    ins = s.activation(dst[:, k, :], src[:, k, :], ACT.Copy, scale=gain[:, col + k:col + k + 1])
                ins.then_inc(tp_hi, 1)

            def sum_squares(name, part, src):
                c = SUMS[name]
                scale = rstd2_mean[:, name[1]:name[1] + 1] if name[0] == "mlppost" else WIDTH[name[0]] ** -0.5
                return s.activation(squares[:, name[1], part * COL:part * COL + src.free_size()], src, ACT.Square,
                                    scale=scale, accum_out=sums[:, part, c:c + 1])

            def sum_x(pos, name, at):
                act.wait_ge(x_loaded[name[1]], 16)
                act.wait_ge(x_ready[name[1]], pos.count(4, at))
                sum_squares(name, 0, x[:, name[1], :]).then_inc(sums_ready, 1)

            def rs(name):
                c = SUMS[name]
                return rstd[:, c:c + 1]

            def wait_rstd(pos, name):
                act.wait_ge(rstd_ready, pos.count(NSUM, SUMS[name] + 1))

            def used(pos, p, per_j=8):
                act.wait_ge(piece_used, pos.count(NP, RING + p + 1, per_j))

            def post_sums(pos, name, p, between=None):
                t = name[1]
                for c in range(2):
                    if t == 0:
                        act.wait_ge(tile0_done, pos.count(4, (0 if name[0] == "mixpost" else 2) + c + 1))
                    else:
                        used(pos, p - 2 + 2 * c)
                    sum_squares(name, c, acc[2 * c + t][:, :]).then_inc(sums_ready, 1)
                    if c == 0 and between is not None:
                        between()

            def relu(pos, j, p, banks):
                used(pos, p)
                for t in range(TT):
                    if j > 0:
                        act.wait_ge(h_ready, pos.count(TT * MJ, TT * (j - 1) + t + 1, TT))
                    s.activation(k_b[:, t, 0:COL], banks[t][:, :], ACT.Relu).then_inc(relu_done, 1)

            def h_hi_of(pos, j, k0, p):
                if p is not None:
                    used(pos, p)
                for b in range(2):
                    act.wait_ge(h_ready, pos.count(TT * MJ, TT * j + b + 1, TT))
                    s.copy(s2_hi[:, k0 + 2 * b:k0 + 2 * b + 2, :], bank_of_h(tok, b)).then_inc(h_hi, 1)

            def exps(pos, i):
                kind, t, g, h, n = QUANTA[i]
                n, w, skip = quantum_shape(i)
                c = q_col(i)
                act.wait_ge(neg_max, pos.count(NQ, i + 1))
                if i >= 2:
                    act.wait_ge(tp_full, pos.count(NF, FILL[("P", i - 2)] + 1))
                for a in range(n):
                    ins = s.activation(probs[:, i % 2, a * w + skip:(a + 1) * w], sc[i % 2][:, a * w + skip:(a + 1) * w],
                                       ACT.Exp, bias=neg_m[:, c + a:c + a + 1], scale=SCALE_A if kind == "A" else SCALE_B,
                                       accum_out=row_sum[:, c + a:c + a + 1])
                ins.then_inc(probs_ready, 1)

            state = [0]
            with act.Fori(0, DEPTH) as l:
                pos = Pos(l)
                state[0] = 0
                act.wait_ge(gains_now, pos.count(1, 1))
                turned_hi(pos, ("x", 0, 0))
                hi(pos, 0)
                turned_hi(pos, ("x", 0, 1))
                hi(pos, 3)
                turned_hi(pos, ("x", 1, 0))
                turned_hi(pos, ("x", 1, 1))
                for t in range(TT):
                    sum_x(pos, ("x", t), 2)
                hi(pos, 6)
                for t in range(TT):
                    act.wait_ge(latent_out, pos.count(2 * TT, t + 1))
                    sum_squares(("cq", t), 0, latent[:, t, 0:BQL]).then_inc(sums_ready, 1)
                hi(pos, 10)
                for t in range(TT):
                    act.wait_ge(latent_out, pos.count(2 * TT, TT + t + 1))
                    sum_squares(("ckv", t), 0, latent[:, t, BQL:BQL + BKL]).then_inc(sums_ready, 1)
                hi(pos, 14)
                used(pos, 11)
                for t in range(TT):
                    if t == 0:
                        s.activation(v_tail[:, :], acc[0][CHUNK:P, AKV * AD:2 * AKV * AD], ACT.Copy,
                                     scale=rstd[CHUNK:P, SUMS[("x", 0)]:SUMS[("x", 0)] + 1])
                    s.activation(kv_a[:, t, :], acc[t][:, 0:2 * AKV * AD], ACT.Copy, scale=rs(("x", t))).then_inc(proj_out, 1)
                turned_hi(pos, ("cq", 0))
                turned_hi(pos, ("cq", 1))
                for c, p in ((0, 15), (1, 19)):
                    hi(pos, p + 3)
                    used(pos, p)
                    for t in range(TT):
                        s.activation(q_of_group(t, c), acc[2 * (1 - c) + t][:, :].rearrange("p (h d) -> p h d", h=AG), ACT.Copy,
                                     scale=rs(("x", t))).then_inc(proj_out, 1)
                    if c == 0:
                        turned_hi(pos, ("ckv",))
                for t in range(TT):
                    wait_rstd(pos, ("ckv", t))
                for c, p in ((0, 21), (1, 23)):
                    hi(pos, p + 3)
                    used(pos, p)
                    for t in range(TT):
                        s.activation(gate_b[:, t, c * BQL:(c + 1) * BQL], acc[2 * (1 - c) + t][:, 0:BQL], ACT.Copy,
                                     scale=rs(("cq", t))).then_inc(proj_out, 1)
                for c, p in ((0, 25), (1, 27)):
                    hi(pos, p + 3 - c)
                    used(pos, p)
                    for t in range(TT):
                        src = acc[2 * (1 - c) + t][:, :].rearrange("p (h d) -> p h d", h=BH // 2)
                        kd = k_b[:, t, :].rearrange("p (h d) -> p h d", h=BH)[:, 4 * c:4 * c + 4, 0:BN]
                        vd = v_b[:, t, :].rearrange("p (h d) -> p h d", h=BH)[:, 4 * c:4 * c + 4, :]
                        s.activation(kd, src[:, :, 0:BN], ACT.Copy, scale=rs(("ckv", t)))
                        s.activation(vd, src[:, :, BN:BN + BV], ACT.Copy, scale=rs(("ckv", t))).then_inc(proj_out, 1)
                for i in range(NSTEP):
                    for name in EXTRA.get(i - 1, []):
                        if name[0] == "y":
                            turned_hi(pos, name)
                    if i % 4 == 0 and 0 < i <= 16:
                        c = i // 4 - 1
                        gt = gate_a if c < 2 else gate_b
                        for t in range(TT):
                            act.wait_ge(gated_out, pos.count(16, 2 * c + t + 1))
                            v = gt[:, t, (c % 2) * COL:(c % 2 + 1) * COL]
                            s.activation(v, v, ACT.Tanh, scale=0.5).then_inc(tanh_done, 1)
                    hi(pos, P_STEP + 3 + i)
                    if i < NQ:
                        exps(pos, i)
                        if i in YLAST[:4]:
                            yi = YLAST.index(i)
                            act.wait_ge(sink_arg, pos.count(4, yi + 1))
                            s.activation(sink_e[:, y_cols(yi)], sink_e[:, y_cols(yi)], ACT.Exp).then_inc(sink_exp, 1)
                p = P_STEP + NSTEP
                hi(pos, p + 4)
                turned_hi(pos, ("y", 5))
                hi(pos, 55 + 1)
                turned_hi(pos, ("mix", 0, 0))
                turned_hi(pos, ("mix", 0, 1))
                hi(pos, 57 + 3)
                turned_hi(pos, ("mix", 1, 0))
                turned_hi(pos, ("mix", 1, 1))
                hi(pos, 63)
                post_sums(pos, ("mixpost", 0), 63)
                hi(pos, 65)
                def first_hi():
                    hi(pos, 66)
                    turned_hi(pos, ("xm", 0, 0))

                post_sums(pos, ("mixpost", 1), 63, between=first_hi)
                turned_hi(pos, ("xm", 0, 1))
                hi(pos, 67)
                turned_hi(pos, ("xm", 1, 0))
                turned_hi(pos, ("xm", 1, 1))
                for t in range(TT):
                    sum_x(pos, ("xm", t), 4)
                hi(pos, 70)
                relu(pos, 0, 67, acc)
                hi(pos, 72)
                for t in range(TT):
                    turned_hi(pos, ("h", t))
                hi(pos, 74)
                relu(pos, 1, 71, sc)
                hi(pos, 79)
                base = 2 * L_LOOP
                assert base == 76
                with act.Fori(0, LOOP_J) as j:
                    here = Pos(l, j)
                    hi(here, base + 4)
                    h_hi_of(here, 1, 0, base - 1)
                    hi(here, base + 6)
                    relu(here, 2, base + 3, sc)
                    hi(here, base + 11)
                base += 8 * LOOP_J
                state[0] = base + 4
                hi(pos, base + 4)
                h_hi_of(pos, MJ - 2, 0, base - 1)
                hi(pos, base + 6)
                relu(pos, MJ - 1, base + 3, sc)
                hi(pos, base + 8)
                h_hi_of(pos, MJ - 1, 4, None)
                hi(pos, NP - 1)
                act.wait_ge(rstd2_ready, pos.count(1, 1))
                post_sums(pos, ("mlppost", 0), NP - 1)
                post_sums(pos, ("mlppost", 1), NP - 1)

        @block.vector
        def _(dve):
            v = nc.vector
            steps = Steps(dve, vec_step)

            dve.sem_inc(lo_ready, 2 * RAW)
            dve.sem_inc(tp_done, 2)
            for t in range(TT):
                dve.sem_inc(x_ready[t], 2)
            dve.wait_ge(freq_ready, 1)
            dve.wait_ge(pos_loaded, 16)
            steps.link(v.tensor_copy(pos_f[:, :], pos_i[:, :]))
            for t in range(TT):
                ins = v.tensor_scalar(ang[:, t, :], freq[:, :], pos_f[:, t:t + 1], None, ALU.mult)
            steps.link(ins)
            magic = 1.5 * 2.0 ** 23
            two_pi = 2 * np.pi
            c1 = 6.28125
            c2 = float(np.floor((two_pi - c1) * 2 ** 20) / 2 ** 20)
            c3 = float(two_pi - c1 - c2)
            pi_in = 3.14159250259
            steps.link(v.tensor_scalar(turns[:, :, :], ang[:, :, :], 1.0 / two_pi, magic, ALU.mult, ALU.add))
            steps.link(v.tensor_scalar(turns[:, :, :], turns[:, :, :], magic, None, ALU.subtract))
            for c in (c1, c2, c3):
                steps.link(v.scalar_tensor_tensor(out=ang[:, :, :], in0=turns[:, :, :], scalar=-c, in1=ang[:, :, :],
                                                  op0=ALU.mult, op1=ALU.add))
            v.tensor_scalar(ang[:, :, :], ang[:, :, :], pi_in, -pi_in, ALU.min, ALU.max).then_inc(angles, 1)

            steps.link(v.memset(gain_all[:, DEPTH, :], 0.0))
            dve.wait_ge(gains_turned, 1)
            for c, n in GAINS:
                ins = v.tensor_copy(gain_all[:, 0:DEPTH, c:c + n],
                                    sc[0][:, DEPTH * c:DEPTH * (c + n)].rearrange("p (l k) -> p l k", l=DEPTH))
            steps.link(ins)
            v.tensor_copy(gain[:, :], gain_all[:, 0, :]).then_inc(gains_now, 1)

            def lo(pos, upto):
                while state[0] <= upto:
                    p = state[0]
                    dve.wait_ge(hi_ready, pos.count(NP, p + 1, 8))
                    v.tensor_tensor(split_view(w_lo, p), raw_view(p), split_view(w_hi, p).bitcast(F32), ALU.subtract)\
                        .then_inc(lo_ready, 1)
                    state[0] += 1

            def turned_lo(pos, name):
                dve.wait_ge(tp_hi, pos.count(NHI, HI_FILL[name] + 1))
                b, kind = bank(name), name[0]
                if kind == "ckv":
                    for t in range(TT):
                        for k in range(KV):
                            i = 2 * t + k
                            ins = v.scalar_tensor_tensor(
                                out=s2_lo[:, KQ + k, t * P:(t + 1) * P], in0=b[:, i * P:(i + 1) * P],
                                scalar=gain[:, G_KVN + k:G_KVN + k + 1],
                                in1=s2_hi[:, KQ + k, t * P:(t + 1) * P].bitcast(F32), op0=ALU.mult, op1=ALU.subtract)
                    ins.then_inc(tp_done, 1)
                    return
                h, low, k0, nk, t = stationary(name)
                dst = low[:, k0:k0 + nk, t * P:(t + 1) * P]
                hiv = h[:, k0:k0 + nk, t * P:(t + 1) * P].bitcast(F32)
                src = b[:, 0:nk * P].rearrange("p (k n) -> p k n", k=nk)
                col = {"x": G_PRE + k0, "xm": G_MLP + k0, "cq": G_QN}.get(kind)
                if kind == "mix":
                    v.scalar_tensor_tensor(out=dst, in0=src, scalar=0.5, in1=hiv, op0=ALU.mult,
                                           op1=ALU.subtract).then_inc(tp_done, 1)
                elif col is None:
                    v.tensor_tensor(dst, src, hiv, ALU.subtract).then_inc(tp_done, 1)
                else:
                    for k in range(nk):
                        ins = v.scalar_tensor_tensor(out=dst[:, k, :], in0=src[:, k, :],
                                                     scalar=gain[:, col + k:col + k + 1], in1=hiv[:, k, :],
                                                     op0=ALU.mult, op1=ALU.subtract)
                    ins.then_inc(tp_done, 1)

            def h_lo_of(pos, j, k0):
                for b in range(2):
                    dve.wait_ge(h_hi, pos.count(TT * (MJ - 1), TT * (j - 1) + b + 1, TT))
                    kk = slice(k0 + 2 * b, k0 + 2 * b + 2)
                    v.tensor_tensor(s2_lo[:, kk, :], bank_of_h(tok, b), s2_hi[:, kk, :].bitcast(F32), ALU.subtract)\
                        .then_inc(h_split, 1)

            def turned_copy(pos, name):
                dve.wait_ge(tp_full, pos.count(NF, FILL[name] + 1))
                b = bank(name)
                if name[0] == "kA":
                    ins = v.tensor_copy(kT_a[:, :], b[:, 0:SEQ])
                elif name[0] == "qA":
                    _, t, h = name
                    ins = v.tensor_copy(qT_a[:, 4 * h:4 * h + 4, t * P:(t + 1) * P],
                                        b[:, :].rearrange("p (h n) -> p h n", h=4))
                elif name[0] in ("qB", "kB"):
                    _, t, h = name
                    dst = qT_b if name[0] == "qB" else kT_b
                    ins = v.tensor_copy(dst[:, 4 * h:4 * h + 4, t * P:(t + 1) * P],
                                        b[0:BQK, :].rearrange("p (h n) -> p h n", h=4))
                else:
                    i = name[1]
                    if i >= 2:
                        dve.wait_ge(pv_done, pos.count(NQ, i - 1))
                    if quantum_shape(i)[2]:
                        v.tensor_copy(probsT[0:CHUNK, i % 2, 0:2 * P], b[0:CHUNK, 0:2 * P])
                        ins = v.tensor_copy(probsT[:, i % 2, 2 * P:4 * P], b[:, 2 * P:4 * P])
                    else:
                        ins = v.tensor_copy(probsT[:, i % 2, :], b[:, :])
                ins.then_inc(tp_done, 1)

            def turned(pos, name):
                turned_lo(pos, name) if name[0] in HI_KINDS else turned_copy(pos, name)

            def used(pos, p):
                dve.wait_ge(piece_used, pos.count(NP, RING + p + 1))

            def rs(name):
                c = SUMS[name]
                return rstd[:, c:c + 1]

            def wait_rstd(pos, name):
                dve.wait_ge(rstd_ready, pos.count(NSUM, SUMS[name] + 1))

            def row_maxima(pos, i):
                kind, t, g, h, n = QUANTA[i]
                n, w, skip = quantum_shape(i)
                c = q_col(i)
                dve.wait_ge(scores_ready, pos.count(NQ, i + 1))
                steps.link(v.tensor_reduce(row_max[:, c:c + n],
                                           sc[i % 2][:, :].rearrange("p (h k) -> p h k", h=n)[:, :, skip:w], AX, ALU.max))
                if kind == "A":
                    v.scalar_tensor_tensor(out=neg_m[:, c:c + n], in0=row_max[:, c:c + n], scalar=-SCALE_A,
                                           in1=neg_sink[:, g * AG + h:g * AG + h + n], op0=ALU.mult,
                                           op1=ALU.min).then_inc(neg_max, 1)
                else:
                    v.tensor_scalar(neg_m[:, c:c + n], row_max[:, c:c + n], -SCALE_B, None, ALU.mult).then_inc(neg_max, 1)
                if i in YLAST[:4]:
                    yi = YLAST.index(i)
                    g = yi % 2
                    dve.wait_ge(neg_max, pos.count(NQ, i + 1))
                    v.tensor_tensor(sink_e[:, y_cols(yi)], neg_m[:, y_cols(yi)], neg_sink[:, g * AG:(g + 1) * AG],
                                    ALU.subtract).then_inc(sink_arg, 1)

            def normalise(pos, yi):
                c = y_cols(yi)
                dve.wait_ge(probs_ready, pos.count(NQ, YLAST[yi] + 1))
                if yi < 4:
                    dve.wait_ge(sink_exp, pos.count(4, yi + 1))
                    steps.link(v.tensor_tensor(denom[:, c], row_sum[:, c], sink_e[:, c], ALU.add))
                    steps.link(v.reciprocal(denom[:, c], denom[:, c]))
                    t, g = yi // 2, yi % 2
                    dst = tok[:, t, g * COL:(g + 1) * COL]
                else:
                    steps.link(v.reciprocal(denom[:, c], row_sum[:, c]))
                    dst = latent[:, yi - 4, 0:COL]
                dve.wait_ge(pv_done, pos.count(NQ, YLAST[yi] + 1))
                v.tensor_tensor(dst.rearrange("p (h d) -> p h d", h=8),
                                acc[2 + yi % 2][:, :].rearrange("p (h d) -> p h d", h=8),
                                denom[:, c].unsqueeze(2).to_broadcast([P, 8, 64]), ALU.mult).then_inc(y_out, 1)

            def gate_logits(pos, c):
                used(pos, P_STEP + 4 * c + 3)
                if c == 0:
                    dve.wait_ge(pool_roped, pos.count(8, 8))
                    dve.wait_ge(bias_loaded, pos.count(16, 16))
                gt = gate_a if c < 2 else gate_b
                for t in range(TT):
                    v.scalar_tensor_tensor(out=gt[:, t, (c % 2) * COL:(c % 2 + 1) * COL], in0=acc[t][:, :],
                                           scalar=rs(("x", t)), in1=bias_g[:, c * COL:(c + 1) * COL],
                                           op0=ALU.mult, op1=ALU.add).then_inc(gated_out, 1)

            def gated(pos, p, gt, c, banks):
                used(pos, p)
                for t in range(TT):
                    view = gt[:, t, c * COL:(c + 1) * COL]
                    v.scalar_tensor_tensor(out=view, in0=view, scalar=1.0, in1=banks[t][:, :], op0=ALU.add,
                                           op1=ALU.mult).then_inc(gated_out, 1)

            def update_x(pos, name, which, between=None):
                t = name[1]
                for c in range(2):
                    dve.wait_ge(sums_ready, pos.count(NPART, SUM_PARTS.index((name, c)) + 1))
                    src, dst, gain_row = acc[2 * c + t][:, :], probs[:, c, :], post_g[:, which, c * COL:(c + 1) * COL]
                    if name[0] == "mlppost":
                        ins = v.scalar_tensor_tensor(out=dst, in0=src, scalar=rstd2[:, t:t + 1], in1=gain_row,
                                                     op0=ALU.mult, op1=ALU.mult)
                    else:
                        ins = v.tensor_tensor(dst, src, gain_row, ALU.mult)
                steps.link(ins)
                if between is not None:
                    between()
                wait_rstd(pos, name)
                for c in range(2):
                    cols = slice(c * COL, (c + 1) * COL)
                    v.scalar_tensor_tensor(out=x[:, t, cols], in0=probs[:, c, :], scalar=rs(name), in1=x[:, t, cols],
                                           op0=ALU.mult, op1=ALU.add).then_inc(x_ready[t], 1)
                dve.wait_ge(x_ready[t], pos.count(4, 4 + 2 * which))

            state = [0]
            with dve.Fori(0, DEPTH) as l:
                pos = Pos(l)
                state[0] = 0
                steps.pos, first = pos, steps.n
                steps.per_layer = 36
                dve.wait_ge(gains_now, pos.count(1, 1))
                lo(pos, 1)
                turned(pos, ("x", 0, 0))
                turned(pos, ("x", 0, 1))
                lo(pos, 3)
                turned(pos, ("x", 1, 0))
                turned(pos, ("x", 1, 1))
                for n0, (c0, N, pair, p) in enumerate(((0, BQL, 0, 3), (BQL, BKL + BR, 1, 7))):
                    lo(pos, p + 3)
                    if n0 == 0:
                        for t in range(TT):
                            wait_rstd(pos, ("x", t))
                    used(pos, p)
                    for t in range(TT):
                        v.tensor_scalar(latent[:, t, c0:c0 + N], acc[2 * pair + t][:, 0:N], rs(("x", t)), None,
                                        ALU.mult).then_inc(latent_out, 1)
                lo(pos, 14)
                turned(pos, ("cq", 0))
                turned(pos, ("cq", 1))
                lo(pos, 18)
                turned(pos, ("ckv",))
                dve.wait_ge(tables_ready, 1)
                for c, p in ((0, 18), (1, 22)):
                    lo(pos, p)
                    dve.wait_ge(proj_out, pos.count(14, 2 * PROJ[f"q{c}"] + 1))
                    rope(v, steps, probs[:, 0, :], q_of_group(0, c).rearrange("p h (c d) -> p h c d", c=2), AG, AD // 2, 0, 1)\
                        .then_inc(roped, 1)
                    dve.wait_ge(roped, pos.count(2, c + 1))
                lo(pos, 25)
                turned(pos, ("kA",))
                turned(pos, ("qA", 0, 0))
                turned(pos, ("qA", 0, 1))
                dve.wait_ge(sinks_loaded, pos.count(16, 16))
                v.tensor_scalar(neg_sink[:, :], sink_in[:, :], -1.0, None, ALU.mult)
                lo(pos, 30)
                for i in range(NSTEP):
                    for name in EXTRA.get(i - 1, []):
                        turned(pos, name)
                    if i < NQ:
                        row_maxima(pos, i)
                    if i >= 2:
                        turned(pos, ("P", i - 2))
                    if i - 3 in YLAST:
                        normalise(pos, YLAST.index(i - 3))
                    if i % 4 == 3 and i < 16:
                        gate_logits(pos, i // 4)
                    lo(pos, P_STEP + 3 + i)
                p = P_STEP + NSTEP
                dve.wait_ge(tanh_done, pos.count(4 * TT, 4 * TT))
                gated(pos, p - 1, gate_a, 0, acc[0:2])
                normalise(pos, 5)
                lo(pos, p + 4)
                turned(pos, ("y", 5))
                lo(pos, 53 + 1)
                gated(pos, 51, gate_b, 0, acc[0:2])
                lo(pos, 55 + 1)
                turned(pos, ("mix", 0, 0))
                turned(pos, ("mix", 0, 1))
                gated(pos, 53, gate_a, 1, sc)
                gated(pos, 55, gate_b, 1, acc[2:4])
                lo(pos, 57 + 3)
                turned(pos, ("mix", 1, 0))
                turned(pos, ("mix", 1, 1))
                lo(pos, 63)
                dve.wait_ge(post_loaded, pos.count(32, 32))
                update_x(pos, ("mixpost", 0), 0)
                lo(pos, 65)
                turned(pos, ("xm", 0, 0))
                update_x(pos, ("mixpost", 1), 0, lambda: turned(pos, ("xm", 0, 1)))
                lo(pos, 67)
                turned(pos, ("xm", 1, 0))
                turned(pos, ("xm", 1, 1))
                dve.wait_ge(tp_done, pos.count(NF, 2 + FILL[("xm", 1, 1)] + 1))
                v.tensor_copy(gain[:, :], gain_all[:, l + 1, :]).then_inc(gains_now, 1)
                lo(pos, 72)
                for t in range(TT):
                    turned(pos, ("h", t))
                lo(pos, 79)
                base = 2 * L_LOOP
                with dve.Fori(0, LOOP_J) as j:
                    here = Pos(l, j)
                    lo(here, base + 4)
                    h_lo_of(here, 1, 0)
                    lo(here, base + 11)
                base += 8 * LOOP_J
                state[0] = base + 4
                lo(pos, base + 4)
                h_lo_of(pos, MJ - 2, 0)
                lo(pos, base + 8)
                h_lo_of(pos, MJ - 1, 4)
                lo(pos, NP - 1)
                dve.wait_ge(rstd2_ready, pos.count(1, 1))
                update_x(pos, ("mlppost", 0), 1)
                update_x(pos, ("mlppost", 1), 1)
                assert steps.n - first == steps.per_layer, steps.n - first

        @block.tensor
        def _(pe):
            mm = nc.tensor.matmul
            pe.sem_inc(piece_used, RING)
            pe.wait_ge(ident_ready, 1)
            pe.wait_ge(gains_loaded, 16 * len(GAINS))
            n = DEPTH * NGAIN
            nc.tensor.transpose(sc[0][:, 0:n], gain_rows[:, :], ident[0:n, 0:n]).then_inc(gains_turned, 1)

            def turn(pos, name, blocks):
                b = bank(name)
                pe.wait_ge(tp_done, pos.count(NF, FILL[name] + 1))
                for i, src in reversed(list(enumerate(blocks))):
                    rows = src.free_size()
                    ins = nc.tensor.transpose(b[0:rows, i * P:(i + 1) * P], src, ident[:, :])
                ins.then_inc(tp_full, 1)

            def turned(pos, name):
                pe.wait_ge(tp_done, pos.count(NF, 2 + FILL[name] + 1))

            def product(pos, p, k0, stat, banks, start=False, stop=False, tiles=(0, 1), release=True, mark=None,
                        free=None):
                a, b = piece_rows(p)
                N = LOADS[p // 2][2]
                h, low = stat
                pe.wait_ge(lo_ready, pos.count(NP, 2 * RAW + p + 1, 8))
                wh = split_view(w_hi, p).rearrange("p (k n) -> p k n", k=b - a)
                wl = split_view(w_lo, p).rearrange("p (k n) -> p k n", k=b - a)
                for t in tiles:
                    if free is not None:
                        free(t)
                    tk = slice(t * P, (t + 1) * P)
                    for k in range(b - a):
                        kk = k0 + a + k
                        mm(banks[t][:, 0:N], h[:, kk, tk], wh[:, k, :], start=(start and k == 0), stop=False)
                        mm(banks[t][:, 0:N], h[:, kk, tk], wl[:, k, :], start=False, stop=False)
                        ins = mm(banks[t][:, 0:N], low[:, kk, tk], wh[:, k, :], start=False,
                                 stop=(stop and k == b - a - 1))
                if release:
                    ins.then_inc(piece_used, 1)
                elif mark is not None:
                    ins.then_inc(mark, 1)

            s1, s2 = (s1_hi, s1_lo), (s2_hi, s2_lo)

            def turn_x(pos, kind, t):
                pe.wait_ge(x_loaded[t], 16)
                for h in range(2):
                    pe.wait_ge(x_ready[t], pos.count(4, (2 if kind == "xm" else 0) + h + 1))
                    turn(pos, (kind, t, h), [x[:, t, (4 * h + k) * P:(4 * h + k + 1) * P] for k in range(4)])

            def first_product(pos, p0, kind, turned0=False):
                N = LOADS[p0 // 2][2]

                def part(t, xs, ws, pieces, first=False, last=False, release=False):
                    for i in pieces:
                        w = split_view(ws, p0 + i).rearrange("p (k n) -> p k n", k=2)
                        if ws is w_lo:
                            pe.wait_ge(lo_ready, pos.count(NP, 2 * RAW + p0 + i + 1))
                        elif xs is s1_hi:
                            if i % 2 == 0:
                                pe.wait_ge(tp_hi, pos.count(NHI, HI_FILL[(kind, t, i // 2)] + 1))
                            pe.wait_ge(hi_ready, pos.count(NP, p0 + i + 1))
                        for k in range(2):
                            ins = mm(acc[t][:, 0:N], xs[:, 2 * i + k, t * P:(t + 1) * P], w[:, k, :],
                                     start=(first and i == 0 and k == 0), stop=(last and i == 3 and k == 1))
                        if release:
                            ins.then_inc(piece_used, 1)

                if not turned0:
                    turn_x(pos, kind, 0)
                part(0, s1_hi, w_hi, range(2), first=True)
                part(0, s1_hi, w_lo, range(2))
                part(0, s1_hi, w_hi, range(2, 4))
                turned(pos, (kind, 0, 1))
                part(0, s1_lo, w_hi, range(4))
                turn_x(pos, kind, 1)
                part(0, s1_hi, w_lo, range(2, 4), last=True)
                part(1, s1_hi, w_hi, range(4), first=True)
                for i in range(4):
                    part(1, s1_hi, w_lo, [i])
                    if i % 2 == 0:
                        turned(pos, (kind, 1, i // 2))
                    part(1, s1_lo, w_hi, [i], last=True, release=True)

            def turn_h0(pos):
                for t in range(TT):
                    pe.wait_ge(h_ready, pos.count(TT * MJ, t + 1))
                    turn(pos, ("h", t), [tok[:, t, k * P:(k + 1) * P] for k in range(4)])

            def scores(pos, i):
                kind, t, g, h, n = QUANTA[i]
                n, w, skip = quantum_shape(i)
                if i >= 2:
                    pe.wait_ge(probs_ready, pos.count(NQ, i - 1))
                r0, r1 = (64 * g, 64 * g + 64) if kind == "A" else (0, P)
                which = 0 if t == 0 else (1 if kind == "A" else 2)
                b = sc[i % 2]
                k0 = w // P - 1 if kind == "B" else 0
                nk = w // P - k0
                view = b[:, :].rearrange("p (h k c) -> p h k c", h=n, c=P)[:, :, k0:, CHUNK:P]
                mk = mask[r0:r1, which, 0:w].rearrange("p (k c) -> p k c", c=P)[:, k0:, CHUNK:P]\
                    .unsqueeze(1).to_broadcast([r1 - r0, n, nk, CHUNK])
                for a in range(n):
                    if kind == "A":
                        q = qT_a[r0:r1, h + a, t * P:(t + 1) * P]
                        k = kT_a[r0:r1, skip:w]
                    else:
                        q = qT_b[:, h + a, t * P:(t + 1) * P]
                        k = kT_b[:, h + a, 0:w]
                    mm(b[:, a * w + skip:(a + 1) * w], q, k, start=(a == 0), stop=False)
                mm(view, chunk_of[r0:r1, :], mk, start=False, stop=True).then_inc(scores_ready, 1)

            def turn_probs(pos, i):
                n, w, skip = quantum_shape(i)
                pe.wait_ge(probs_ready, pos.count(NQ, i + 1))
                blocks = []
                for b in range(w // P):
                    for a in range(n):
                        blocks.append(probs[:, i % 2, a * w + b * P + (skip if b == 0 else 0):a * w + (b + 1) * P])
                turn(pos, ("P", i), blocks)

            def values(pos, i):
                kind, t, g, h, n = QUANTA[i]
                n, w, skip = quantum_shape(i)
                yi = first_of_y(i)
                turned(pos, ("P", i))
                if i == 0 or i - 1 in YLAST:
                    if yi >= 2:
                        pe.wait_ge(y_out, pos.count(NY, yi - 1))
                y = acc[2 + yi % 2]
                for a in range(n):
                    for b in range(w // P):
                        rows = CHUNK if (skip and b == 0) else P
                        pt = probsT[0:rows, i % 2, (b * n + a) * P:(b * n + a + 1) * P]
                        if kind == "A":
                            vv = v_tail[:, g * AD:(g + 1) * AD] if rows == CHUNK else \
                                kv_a[:, b, (AKV + g) * AD:(AKV + g + 1) * AD]
                        else:
                            vv = v_b[:, b, (h + a) * BV:(h + a + 1) * BV]
                        ins = mm(y[:, (h + a) * 64:(h + a + 1) * 64], pt, vv, start=(b == 0), stop=(b == w // P - 1))
                ins.then_inc(pv_done, 1)

            def extra(pos, name):
                if name[0] == "qA":
                    _, t, h = name
                    blocks = [tok[:, t, (4 * h + a) * AKV * AD:(4 * h + a + 1) * AKV * AD] for a in range(4)]
                elif name[0] in ("qB", "kB"):
                    _, t, h = name
                    src = gate_b if name[0] == "qB" else k_b
                    blocks = [src[:, t, (4 * h + a) * BQK:(4 * h + a + 1) * BQK] for a in range(4)]
                else:
                    yi = name[1]
                    pe.wait_ge(y_out, pos.count(NY, yi + 1))
                    src = tok[:, yi // 2, (yi % 2) * COL:(yi % 2 + 1) * COL] if yi < 4 else latent[:, yi - 4, 0:COL]
                    blocks = [src[:, k * P:(k + 1) * P] for k in range(4)]
                turn(pos, name, blocks)

            def projected(pos, name):
                return lambda t: pe.wait_ge(proj_out, pos.count(14, 2 * PROJ[name] + t + 1))

            def gate_free(pos, name):
                return lambda t: pe.wait_ge(gated_out, pos.count(16, 2 * GATED[name] + t + 1))

            pair = [acc[0:2], acc[2:4]]
            with pe.Fori(0, DEPTH) as l:
                pos = Pos(l)
                first_product(pos, 0, "x")
                for i, p in enumerate(range(4, 8)):
                    product(pos, p, 4 * (i // 2), s1, pair[1], i == 0, i == 3)
                def latent_free(n):
                    return lambda t: pe.wait_ge(latent_out, pos.count(2 * TT, n * TT + t + 1))

                for i, p in enumerate(range(8, 12)):
                    product(pos, p, 4 * (i // 2), s1, pair[0], i == 0, i == 3, free=latent_free(0) if i == 0 else None)
                for t in range(TT):
                    pe.wait_ge(latent_out, pos.count(2 * TT, t + 1))
                    turn(pos, ("cq", t), [latent[:, t, k * P:(k + 1) * P] for k in range(KQ)])
                for i, p in enumerate(range(12, 16)):
                    product(pos, p, 4 * (i // 2), s1, pair[1], i == 0, i == 3, free=latent_free(1) if i == 0 else None)
                turn(pos, ("ckv",), [latent[:, t, BQL + k * P:BQL + (k + 1) * P] for t in range(TT) for k in range(KV)])
                for i, p in enumerate(range(16, 20)):
                    product(pos, p, 4 * (i // 2), s1, pair[0], i == 0, i == 3, free=projected(pos, "kv") if i == 0 else None)
                turned(pos, ("ckv",))
                for c, (q, before, k0) in enumerate((("uq0", "q0", 0), ("uq1", "q1", 0), ("ukv0", "uq0", KQ), ("ukv1", "uq1", KQ))):
                    if c == 2:
                        pe.wait_ge(pool_roped, pos.count(8, 2 * POOL_ROPED["kA"] + 2))
                        turn(pos, ("kA",), [kv_a[:, t, 0:AKV * AD] for t in range(TT)])
                        pe.wait_ge(roped, pos.count(2, 2))
                        extra(pos, ("qA", 0, 0))
                        extra(pos, ("qA", 0, 1))
                    for i in range(2):
                        product(pos, 20 + 2 * c + i, k0, s2, pair[1 - c % 2], i == 0, i == 1,
                                free=projected(pos, before) if i == 0 else None)
                turned(pos, ("qA", 0, 1))
                pe.wait_ge(consts_ready, 2)
                for i in range(NSTEP):
                    if i < NQ:
                        scores(pos, i)
                    if i >= 2:
                        turn_probs(pos, i - 2)
                    p, free = P_STEP + i, None
                    if i % 4 == 0:
                        free = projected(pos, "ukv1") if i == 0 else gate_free(pos, f"g{i // 4 - 1}")
                    if i < 16:
                        product(pos, p, 4 * (i % 4 // 2), s1, pair[0], i % 4 == 0, i % 4 == 3, free=free)
                    else:
                        if i in (16, 18):
                            turned(pos, ("y", 2 if i == 16 else 3))
                        product(pos, p, 4 * (i % 4 // 2), s2, pair[0], i % 4 == 0, i % 4 == 3, free=free)
                    if i >= 2:
                        values(pos, i - 2)
                    for name in EXTRA.get(i, []):
                        if i in (1, 3):
                            pe.wait_ge(pool_roped, pos.count(8, 6 if i == 1 else 8))
                        extra(pos, name)
                product(pos, 48, 0, s2, sc, True, False)
                extra(pos, ("y", 5))
                product(pos, 49, 0, s2, sc)
                turned(pos, ("y", 5))
                product(pos, 50, 4, s1, pair[0], True, False, free=gate_free(pos, "oa0"))
                product(pos, 51, 4, s1, pair[0], False, True)
                product(pos, 52, 4, s2, sc)
                product(pos, 53, 4, s2, sc, False, True)
                for t in range(TT):
                    pe.wait_ge(mixed, pos.count(4, t + 1))
                    turn(pos, ("mix", 0, t), [tok[:, t, k * P:(k + 1) * P] for k in range(4)])
                product(pos, 54, 4, s1, pair[1], True, False)
                product(pos, 55, 4, s1, pair[1], False, True)
                turned(pos, ("mix", 0, 1))
                product(pos, 56, 0, s1, pair[0], True)
                product(pos, 57, 0, s1, pair[0])
                for t in range(TT):
                    pe.wait_ge(mixed, pos.count(4, 2 + t + 1))
                    turn(pos, ("mix", 1, t), [tok[:, t, COL + k * P:COL + (k + 1) * P] for k in range(4)])
                product(pos, 58, 0, s1, pair[1], True)
                product(pos, 59, 0, s1, pair[1])
                turned(pos, ("mix", 1, 1))

                def finish(pos, p, k0, stat, before_last=None):
                    for t in range(TT):
                        for i in range(4):
                            if t == 1 and i == 3 and before_last is not None:
                                before_last()
                            product(pos, p + i, k0, stat, pair[i // 2], False, i % 2 == 1, tiles=(t,), release=(t == 1),
                                    mark=tile0_done if i % 2 == 1 else None)

                finish(pos, 60, 4, s1, lambda: turn_x(pos, "xm", 0))

                def mlp_in(pos, p, between=None):
                    for i in range(4):
                        if i == 2 and between is not None:
                            between()
                        pe.wait_ge(lo_ready, pos.count(NP, 2 * RAW + p + i + 1, 8))
                        wh, wl = (split_view(w, p + i).rearrange("p (k n) -> p k n", k=2) for w in (w_hi, w_lo))
                        for f in range(4):
                            out, cols = sc[f // 2][:, (f % 2) * SEQ:(f % 2 + 1) * SEQ], slice(f * P, (f + 1) * P)
                            for k in range(2):
                                kk = 2 * i + k
                                mm(out, wh[:, k, cols], s1_hi[:, kk, :], start=(i == 0 and k == 0 and f % 2 == 0), stop=False)
                                mm(out, wh[:, k, cols], s1_lo[:, kk, :], start=False, stop=False)
                                ins = mm(out, wl[:, k, cols], s1_hi[:, kk, :], start=False, stop=(i == 3 and k == 1 and f % 2 == 1))
                        ins.then_inc(piece_used, 1)

                def h_is_split(pos, j):
                    pe.wait_ge(h_split, pos.count(TT * (MJ - 1), TT * j, TT))

                def mlp_out(pos, p, start=False):
                    for i in range(4):
                        product(pos, p + i, 0, s2, pair[i // 2], start and i % 2 == 0)

                first_product(pos, 2 * L_MLP, "xm", turned0=True)
                mlp_in(pos, 68, lambda: turn_h0(pos))
                turned(pos, ("h", 1))
                mlp_out(pos, 72, start=True)
                with pe.Fori(0, LOOP_J) as j:
                    here = Pos(l, j)
                    pe.wait_ge(relu_done, here.count(TT * MJ, 2 * TT, TT))
                    mlp_in(here, 76)
                    h_is_split(here, 1)
                    mlp_out(here, 80)
                base = 2 * L_LOOP + 8 * LOOP_J
                pe.wait_ge(relu_done, pos.count(TT * MJ, TT * (MJ - 1)))
                mlp_in(pos, base)
                h_is_split(pos, MJ - 2)
                for i in range(4):
                    product(pos, base + 4 + i, 0, s2, pair[i // 2])
                h_is_split(pos, MJ - 1)
                finish(pos, base + 8, 4, s2)


_INS = ["x", "positions", "g_mix_pre", "g_mix_post", "g_mlp_pre", "g_mlp_post", "w_in", "b_gate", "sinks",
        "q_norm", "kv_norm", "w_uq", "w_ukv", "w_oa", "w_ob", "w_out", "w_mlp_in", "w_mlp_out"]


def kernel(**inputs):
    import concourse.bacc as bacc
    from concourse.bass_utils import run_bass_kernel_spmd

    nc = bacc.Bacc("TRN2", target_bir_lowering=False, num_devices=1)
    arrays, args = {}, []
    for name in _INS:
        a = np.ascontiguousarray(inputs[name])
        arrays["in_" + name] = a
        args.append(nc.dram_tensor("in_" + name, a.shape, mybir.dt.from_np(a.dtype), kind="ExternalInput").ap())
    out = nc.dram_tensor("out_x", (1, SEQ, D), F32, kind="ExternalOutput").ap()
    build(nc, *args, out)
    result = run_bass_kernel_spmd(nc, [arrays], core_ids=[0])
    return result.results[0]["out_x"]
```
